# Optimizing a Trainium2 kernel written in Bass

```python
import jax, jax.numpy as jnp
from jax import lax
import numpy as np

D_MODEL = 1024
BATCH = 1
SEQ = 512
DEPTH = 1

A_HEADS = 8
A_HEAD_DIM = 128
A_WIDTH = A_HEADS * A_HEAD_DIM
IDX_HEADS = 8
IDX_DIM = 64
TOPK_MAX = 256
Q_BLOCK = 64
B_HEADS = 8
B_KEY_DIM = 128
B_VAL_DIM = 128
B_QK_WIDTH = B_HEADS * B_KEY_DIM
B_V_WIDTH = B_HEADS * B_VAL_DIM
CONV_WIDTH = 4
CHUNK = 64
ROPE_THETA = 500000.0
ROPE_FRACTION = 4
EPS = 1e-6
SPLIT_SIZES = (A_WIDTH, A_WIDTH, A_WIDTH, A_WIDTH,
               IDX_HEADS * IDX_DIM, IDX_DIM, IDX_HEADS,
               B_QK_WIDTH, B_QK_WIDTH, B_V_WIDTH, B_V_WIDTH, B_HEADS, B_HEADS,
               D_MODEL, D_MODEL)
D_IN = 4 * A_WIDTH + IDX_HEADS * IDX_DIM + IDX_DIM + IDX_HEADS + 2 * B_QK_WIDTH + 2 * B_V_WIDTH + 2 * B_HEADS + 2 * D_MODEL

kernel_name = "hybrid_dsa_gdn_gated_merge_block"

def rmsnorm(x, gain):
    xf = x.astype(jnp.float32)
    y = xf * lax.rsqrt(jnp.mean(xf * xf, axis=-1, keepdims=True) + EPS)
    return (y * gain.astype(jnp.float32)).astype(x.dtype)

def layernorm(x, gain, bias):
    xf = x.astype(jnp.float32)
    mu = jnp.mean(xf, axis=-1, keepdims=True)
    var = jnp.mean(jnp.square(xf - mu), axis=-1, keepdims=True)
    y = (xf - mu) * lax.rsqrt(var + EPS)
    return (y * gain.astype(jnp.float32) + bias.astype(jnp.float32)).astype(x.dtype)

def l2norm(x):
    xf = x.astype(jnp.float32)
    return xf * lax.rsqrt(jnp.sum(xf * xf, axis=-1, keepdims=True) + EPS)

def partial_rope(x, positions):
    d = x.shape[-1]
    rot = d // ROPE_FRACTION
    half = rot // 2
    inv_freq = ROPE_THETA ** (-(jnp.arange(half, dtype=jnp.float32) * 2.0 / rot))
    ang = positions.astype(jnp.float32)[..., None] * inv_freq
    cos = jnp.cos(ang)[:, :, None, :].astype(x.dtype)
    sin = jnp.sin(ang)[:, :, None, :].astype(x.dtype)
    x1, x2, rest = x[..., :half], x[..., half:rot], x[..., rot:]
    return jnp.concatenate([x1 * cos - x2 * sin, x2 * cos + x1 * sin, rest], axis=-1)

def dsa_attention(q, k, v, q_idx, k_idx, w_idx):
    b, s, h, dh = q.shape
    topk = min(TOPK_MAX, s // 4)
    nb = s // Q_BLOCK

    def to_blocks(t):
        return jnp.swapaxes(t.reshape((b, nb, Q_BLOCK) + t.shape[2:]), 0, 1)

    tpos = jnp.arange(s, dtype=jnp.int32).reshape(nb, Q_BLOCK)
    key_pos = jnp.arange(s, dtype=jnp.int32)
    gather = jax.vmap(lambda kk, ii: kk[ii])

    def block(args):
        qb, qib, wb, tb = args
        logits = jnp.einsum('bqhd,bsd->bqhs', qib, k_idx) * (IDX_DIM ** -0.5)
        score = jnp.einsum('bqh,bqhs->bqs', wb, jax.nn.relu(logits)) * (IDX_HEADS ** -0.5)
        causal = key_pos[None, :] <= tb[:, None]
        score = jnp.where(causal[None], score.astype(jnp.float32), -jnp.inf)
        _, idx = lax.top_k(score, topk)
        valid = idx <= tb[None, :, None]
        k_sel = gather(k, idx)
        v_sel = gather(v, idx)
        att = jnp.einsum('bqhd,bqkhd->bhqk', qb, k_sel).astype(jnp.float32) * (dh ** -0.5)
        att = jnp.where(valid[:, None], att, -jnp.inf)
        p = jax.nn.softmax(att, axis=-1).astype(v.dtype)
        return jnp.einsum('bhqk,bqkhd->bqhd', p, v_sel)

    out = lax.map(block, (to_blocks(q), to_blocks(q_idx), to_blocks(w_idx), tpos))
    return jnp.swapaxes(out, 0, 1).reshape(b, s, h, dh)

def causal_depthwise_conv(x, w):
    ch = x.shape[-1]
    return lax.conv_general_dilated(x, w[:, None, :].astype(x.dtype), window_strides=(1,),
                                    padding=[(CONV_WIDTH - 1, 0)],
                                    dimension_numbers=('NWC', 'WIO', 'NWC'),
                                    feature_group_count=ch)

def gated_delta_rule_chunked(q, k, v, g, beta):
    b, s, h, dk = q.shape
    dv = v.shape[-1]
    n = s // CHUNK
    f32 = jnp.float32

    def chunks(t):
        t = jnp.moveaxis(t.astype(f32), 2, 1)
        return t.reshape((b, h, n, CHUNK) + t.shape[3:])

    qc, kc, vc, gch, bc = chunks(q), chunks(k), chunks(v), chunks(g), chunks(beta)
    gc = jnp.cumsum(gch, axis=-1)
    ii = jnp.arange(CHUNK)
    incl = ii[:, None] >= ii[None, :]
    strict = ii[:, None] > ii[None, :]
    decay = jnp.exp(jnp.where(incl, gc[..., :, None] - gc[..., None, :], -jnp.inf))
    kb = kc * bc[..., None]
    vb = vc * bc[..., None]
    lower = jnp.where(strict, jnp.einsum('bhncd,bhnjd->bhncj', kb, kc) * decay, 0.0)
    eye = jnp.eye(CHUNK, dtype=f32)
    t_mat = lax.linalg.triangular_solve(lower + eye, jnp.broadcast_to(eye, lower.shape),
                                        left_side=True, lower=True, unit_diagonal=True)
    u = jnp.einsum('bhncj,bhnjv->bhncv', t_mat, vb)
    w = jnp.einsum('bhncj,bhnjd->bhncd', t_mat, kb * jnp.exp(gc)[..., None])
    intra = jnp.einsum('bhncd,bhnjd->bhncj', qc, kc) * decay

    def step(state, xs):
        q_n, k_n, u_n, w_n, g_n, a_n = xs
        v_new = u_n - jnp.einsum('bhcd,bhdv->bhcv', w_n, state)
        o = (jnp.einsum('bhcd,bhdv->bhcv', q_n * jnp.exp(g_n)[..., None], state)
             + jnp.einsum('bhcj,bhjv->bhcv', a_n, v_new))
        g_last = g_n[..., -1]
        state = (state * jnp.exp(g_last)[..., None, None]
                 + jnp.einsum('bhcd,bhcv->bhdv', k_n * jnp.exp(g_last[..., None] - g_n)[..., None], v_new))
        return state, o

    xs = tuple(jnp.moveaxis(t, 2, 0) for t in (qc, kc, u, w, gc, intra))
    state0 = jnp.zeros((b, h, dk, dv), f32)
    _, o = lax.scan(step, state0, xs)
    o = jnp.moveaxis(o, 0, 2).reshape(b, h, s, dv)
    return jnp.moveaxis(o, 1, 2).astype(v.dtype)

def hybrid_layer(x, c, positions, w_ada, b_ada, pre_norm_gain, post_norm_gain, w_in,
                 idx_k_ln_gain, idx_k_ln_bias, dn_conv_w, dn_a_log, dn_dt_bias, dn_norm_gain,
                 w_a_out, w_b_out, w_o):
    b, s, _ = x.shape
    mod = c @ w_ada + b_ada
    shift, scale, gate = jnp.split(mod, 3, axis=-1)
    h = rmsnorm(x, pre_norm_gain) * (1.0 + scale[:, None, :]) + shift[:, None, :]
    proj = h @ w_in
    points = list(np.cumsum(SPLIT_SIZES)[:-1])
    (aq, ak, av, az, iq, ik, iw, bq, bk, bv, bz, bbeta, ba, ga, gb) = jnp.split(proj, points, axis=-1)

    qa = partial_rope(aq.reshape(b, s, A_HEADS, A_HEAD_DIM), positions)
    ka = partial_rope(ak.reshape(b, s, A_HEADS, A_HEAD_DIM), positions)
    va = av.reshape(b, s, A_HEADS, A_HEAD_DIM)
    q_idx = partial_rope(iq.reshape(b, s, IDX_HEADS, IDX_DIM), positions)
    k_idx = partial_rope(layernorm(ik, idx_k_ln_gain, idx_k_ln_bias)[:, :, None, :], positions)[:, :, 0, :]
    o_a = dsa_attention(qa, ka, va, q_idx, k_idx, iw).reshape(b, s, A_WIDTH)
    y_a = (o_a * jax.nn.silu(az)) @ w_a_out

    qkv = jax.nn.silu(causal_depthwise_conv(jnp.concatenate([bq, bk, bv], axis=-1), dn_conv_w))
    cq, ck, cv = jnp.split(qkv, [B_QK_WIDTH, 2 * B_QK_WIDTH], axis=-1)
    qb = l2norm(cq.reshape(b, s, B_HEADS, B_KEY_DIM)) * (B_KEY_DIM ** -0.5)
    kb = l2norm(ck.reshape(b, s, B_HEADS, B_KEY_DIM))
    vb = cv.reshape(b, s, B_HEADS, B_VAL_DIM)
    beta = jax.nn.sigmoid(bbeta.astype(jnp.float32))
    g = -jnp.exp(dn_a_log.astype(jnp.float32)) * jax.nn.softplus(ba.astype(jnp.float32) + dn_dt_bias.astype(jnp.float32))
    o_b = gated_delta_rule_chunked(qb, kb, vb, g, beta)
    o_b = rmsnorm(o_b, dn_norm_gain) * jax.nn.silu(bz.reshape(b, s, B_HEADS, B_VAL_DIM))
    y_b = o_b.reshape(b, s, B_V_WIDTH) @ w_b_out

    y = jax.nn.sigmoid(ga) * y_a + jax.nn.sigmoid(gb) * y_b
    out = y @ w_o
    return x + gate[:, None, :] * rmsnorm(out, post_norm_gain)

def setup_inputs(seed: int = 0) -> dict:
    key = jax.random.key(seed)
    ks = jax.random.split(key, 20)
    nrm = jax.random.normal
    d = D_MODEL
    conv_ch = 2 * B_QK_WIDTH + B_V_WIDTH
    dt = jnp.exp(jax.random.uniform(ks[10], (DEPTH, B_HEADS), minval=np.log(1e-3), maxval=np.log(1e-1)))
    return {
        "x": nrm(ks[0], (BATCH, SEQ, d), jnp.float32),
        "c": nrm(ks[1], (BATCH, d), jnp.float32),
        "positions": (jnp.arange(SEQ, dtype=jnp.int32)[None, :]
                      + jax.random.randint(ks[2], (BATCH, 1), 0, 1024, dtype=jnp.int32)),
        "w_ada": nrm(ks[3], (DEPTH, d, 3 * d), jnp.float32) * (0.5 * d ** -0.5),
        "b_ada": nrm(ks[4], (DEPTH, 3 * d), jnp.float32) * 0.01,
        "pre_norm_gain": 1.0 + 0.05 * nrm(ks[5], (DEPTH, d), jnp.float32),
        "post_norm_gain": 1.0 + 0.05 * nrm(ks[6], (DEPTH, d), jnp.float32),
        "w_in": nrm(ks[7], (DEPTH, d, D_IN), jnp.float32) * d ** -0.5,
        "idx_k_ln_gain": 1.0 + 0.05 * nrm(ks[8], (DEPTH, IDX_DIM), jnp.float32),
        "idx_k_ln_bias": 0.02 * nrm(ks[9], (DEPTH, IDX_DIM), jnp.float32),
        "dn_conv_w": nrm(ks[11], (DEPTH, CONV_WIDTH, conv_ch), jnp.float32) * CONV_WIDTH ** -0.5,
        "dn_a_log": jnp.log(jax.random.uniform(ks[12], (DEPTH, B_HEADS), minval=1.0, maxval=16.0)),
        "dn_dt_bias": dt + jnp.log(-jnp.expm1(-dt)),
        "dn_norm_gain": 1.0 + 0.05 * nrm(ks[13], (DEPTH, B_VAL_DIM), jnp.float32),
        "w_a_out": nrm(ks[14], (DEPTH, A_WIDTH, d), jnp.float32) * A_WIDTH ** -0.5,
        "w_b_out": nrm(ks[15], (DEPTH, B_V_WIDTH, d), jnp.float32) * B_V_WIDTH ** -0.5,
        "w_o": nrm(ks[16], (DEPTH, d, d), jnp.float32) * d ** -0.5,
    }

def reference(x, c, positions, w_ada, b_ada, pre_norm_gain, post_norm_gain, w_in,
              idx_k_ln_gain, idx_k_ln_bias, dn_conv_w, dn_a_log, dn_dt_bias, dn_norm_gain,
              w_a_out, w_b_out, w_o):
    for layer in range(DEPTH):
        x = hybrid_layer(x, c, positions, w_ada[layer], b_ada[layer], pre_norm_gain[layer],
                         post_norm_gain[layer], w_in[layer], idx_k_ln_gain[layer], idx_k_ln_bias[layer],
                         dn_conv_w[layer], dn_a_log[layer], dn_dt_bias[layer], dn_norm_gain[layer],
                         w_a_out[layer], w_b_out[layer], w_o[layer])
    return x


_drawn_inputs = setup_inputs


def setup_inputs(seed=0):
    import zlib

    import numpy as np

    out = dict(_drawn_inputs(seed))
    spreads = {}
    factors = {'b_ada': 3.62, 'idx_k_ln_gain': 4.176, 'idx_k_ln_bias': 6.978, 'dn_norm_gain': 2.752}
    for name, (base, spread) in spreads.items():
        noise = np.random.default_rng([zlib.crc32(name.encode()), seed]).standard_normal(out[name].shape)
        drawn = base * np.exp(spread * noise) if base else spread * noise
        out[name] = __import__('jax').numpy.asarray(drawn.astype(out[name].dtype))
    for name, factor in factors.items():
        out[name] = (out[name] * factor).astype(out[name].dtype)
    return out
```

```python
from contextlib import ExitStack

import numpy as np

import concourse.bass as bass
from concourse import mybir

ALU = mybir.AluOpType
ACT = mybir.ActivationFunctionType
AX_X = mybir.AxisListType.X
F32 = mybir.dt.float32
F32R = mybir.dt.float32r
BF16 = mybir.dt.bfloat16
I32 = mybir.dt.int32

P = 128
D = 1024
S = 512
KT = D // P
NT = S // P
HEADS = 8
HD = 128
IDX_HEADS, IDX_DIM = 8, 64
TOPK = min(256, S // 4)
CONV = 4
THETA = 500000.0
EPS = 1e-6
AW = HEADS * HD
COL_AQ, COL_AK, COL_AV, COL_AZ = 0, AW, 2 * AW, 3 * AW
COL_IQ = 4 * AW
COL_IK = COL_IQ + IDX_HEADS * IDX_DIM
COL_BQ = COL_IK + IDX_DIM + IDX_HEADS
COL_BK, COL_BV, COL_BZ = COL_BQ + AW, COL_BQ + 2 * AW, COL_BQ + 3 * AW
COL_BETA = COL_BQ + 4 * AW
COL_GA = COL_BETA + 2 * HEADS
COL_GB = COL_GA + D
D_IN = COL_GB + D
N_SMALL = IDX_DIM + IDX_HEADS + 2 * HEADS
SM_IW, SM_BETA, SM_DECAY = IDX_DIM, IDX_DIM + IDX_HEADS, IDX_DIM + IDX_HEADS + HEADS

FILL = -1.0e38
TAKEN = -3.0e38
MASKED = -1.0e30

LEVELS = [1, 2, 4, 8, 16, 32, 64]
(C_ID, C_TRIU, C_LOW, C_TRIL, C_FILL, C_MASKED, C_ONES, C_NEG1LOW, C_NEG) = range(9)
N_CST = C_NEG + len(LEVELS)
R_CONV, R_GAIN, R_BADA, R_C = 0, CONV * 24, CONV * 24 + 8, CONV * 24 + 24
R2_LNG, R2_LNB, R2_NG = 0, 1, 2

U_SMALL, U_IQ, U_GATE, U_LOOP = 0, 1, 5, 13
Q_LOOP = 5
ITERS = 3 * 8
Q_OUT = Q_LOOP + 4 * ITERS
U_OUT = U_LOOP + 4 * ITERS
RING = 4
OUT_COLS = [0, 128, 384, 256, 512, 640, 896, 768]
ROUNDS = 16


def constants():
    p = np.arange(P)[:, None]
    f = np.arange(P)[None, :]
    cst = np.zeros((P, N_CST, P), np.float32)
    cst[:, C_ID] = p == f
    cst[:, C_TRIU] = p <= f
    cst[:, C_LOW] = p > f
    cst[:, C_TRIL] = p >= f
    cst[:, C_FILL] = np.where(f > p, np.float32(FILL), 0)
    cst[:, C_MASKED] = np.where(f > p, np.float32(MASKED), 0)
    cst[:, C_ONES] = 1.0
    for n, s in enumerate(LEVELS):
        cst[:, C_NEG + n] = -1.0 * ((p // s % 2 == 0) & (f // s == p // s + 1))
    cst[:, C_NEG1LOW] = cst[:, C_NEG].T
    cols = np.zeros((P, 4), np.float32)
    for n, (rot, group) in enumerate(((HD // 4, P), (IDX_DIM // 4, IDX_DIM))):
        half = rot // 2
        i = np.arange(P) % group
        freq = np.float32(THETA) ** (-(np.arange(half, dtype=np.float32) * np.float32(2.0) / np.float32(rot)))
        cols[:, n] = np.where(i < rot, freq[i % half], 0.0)
        cols[:, 2 + n] = np.where(i < half, -1.0, 1.0)
    return cst, cols


class Steps:

    def __init__(self, sem, steps, ahead=0):
        self.sem, self.steps, self.made, self.ahead = sem, list(steps), 0, ahead
        assert len(set(self.steps)) == len(self.steps)

    def at(self, step, h=0):
        return self.sem, (h + self.ahead) * len(self.steps) + (self.steps.index(step) + 1)

    def count_ahead(self, eng):
        eng.sem_inc(self.sem, self.ahead * len(self.steps))

    def inc(self, step):
        assert self.steps[self.made % len(self.steps)] == step, (step, self.steps[self.made % len(self.steps)])
        self.made += 1
        return self.sem, 1


def before_first(h):
    return isinstance(h, int) and h < 0


def build(nc, x, c, positions, w_ada, b_ada, pre_gain, post_gain, w_in, ln_gain, ln_bias, conv_w, a_log, dt_bias,
          norm_gain, w_a_out, w_b_out, w_o, cst_in, cols_in, out):
    with ExitStack() as ctx:
        program(nc, ctx, x, c, positions, w_ada, b_ada, pre_gain, post_gain, w_in, ln_gain, ln_bias, conv_w, a_log,
                dt_bias, norm_gain, w_a_out, w_b_out, w_o, cst_in, cols_in, out)


def program(nc, ctx, x, c, positions, w_ada, b_ada, pre_gain, post_gain, w_in, ln_gain, ln_bias, conv_w, a_log,
            dt_bias, norm_gain, w_a_out, w_b_out, w_o, cst_in, cols_in, out):
    cursor = [-(-nc.sbuf_base // 64) * 64]

    def place(name, shape, dt=F32, at=None):
        size = int(np.prod(shape[1:])) * (2 if dt == BF16 else 4)
        size = -(-size // 64) * 64
        if at is None:
            at = cursor[0]
            cursor[0] += size
        t = nc.alloc_sbuf_tensor_at(name, list(shape), dt, offset=at)
        ends[name] = at + size
        return t

    ends = {}
    cst_at = cursor[0]
    cst = place("cst", [P, N_CST, P])
    cols = place("cols", [P, 4])
    pcol = place("pcol", [P, 2, P])
    small_cols = place("small_cols", [P, 64])
    cb = place("cb", [P, KT, P])
    gate = place("gate", [P, D])
    tab_at = cursor[0]
    tab_sin = place("tab_sin", [P, 2, S])
    tab_cos = place("tab_cos", [P, 2, S])
    gsc = place("gsc", [P, 10, NT, HEADS])
    nhalf = place("nhalf", [P, 8])
    eps_k = place("eps_k", [P, 8])
    eps_o = place("eps_o", [P, 4])
    h_at = cursor[0]
    h_hi = place("h_hi", [P, KT, S], F32R)
    h_lo = place("h_lo", [P, KT, S], F32R)
    raw = place("raw", [P, RING, KT, P])
    w_hi_at = cursor[0]
    w_hi = place("w_hi", [P, RING, KT, P], F32R)
    w_lo_at = cursor[0]
    w_lo = place("w_lo", [P, RING, KT, P], F32R)
    base = cursor[0]
    ob = place("ob", [P, HEADS, S])
    score = place("score", [P, NT, S])
    par0 = cursor[0]
    U = place("U", [P, 2, NT, P])
    vb = place("vb", [P, 2, NT, P])
    kd = place("kd", [P, 2, NT, P])
    intra = place("intra", [P, 2, NT, P])
    qe = place("qe", [P, 2, S])
    kbe = place("kbe", [P, 2, NT, P])
    zb_at = cursor[0]
    zb = place("zb", [P, 2, S])
    work0 = cursor[0]
    rows = place("rows", [P, 3, 3 + S + 1])
    y3 = place("y3", [P, 3, S])
    yy_at = cursor[0]
    yy = place("yy", [P, 2, NT, P])
    kn = place("kn", [P, NT, P])
    kT = place("kT", [P, S])
    E = place("E", [P, S])
    L = place("L", [P, NT, P])
    T = place("T", [P, NT, P])
    after_solve = cursor[0]
    zraw_at = cursor[0]
    zraw = place("zraw", [P, S])
    tz = place("tz", [P, S])
    wTn_at = cursor[0]
    wTn = place("wTn", [P, S])
    o_tok = place("o_tok", [P, NT, P])
    state = place("state", [P, P])
    vnew = place("vnew", [P, P])
    junk = place("junk", [P, 12 * P], BF16)
    qk_at = cursor[0]
    qk = place("qk", [P, 2, S])
    vT = place("vT", [P, S])
    end = cursor[0]
    m8 = place("m8", [P, 3, 8])
    st8 = place("st8", [P, 2, 8])
    sst = place("sst", [P, 2, 8])
    fo = place("fo", [P, 3, 4])
    amx = place("amx", [P, 4, 4])
    assert cursor[0] <= nc.sbuf_usable_end, (cursor[0], nc.sbuf_usable_end)
    cursor[0] = work0
    sw = place("sw", [32, 2, S])
    Vt = place("Vt", [P, NT, P])
    prob = place("prob", [P, NT, S])
    probT = place("probT", [P, NT, S])
    assert cursor[0] <= after_solve
    oa = place("oa", [P, HEADS, S], at=par0)
    cursor[0] = par0 + HEADS * S * 4
    oa_hi = place("oa_hi", [P, HEADS, S], F32R)
    oa_lo = place("oa_lo", [P, HEADS, S], F32R)
    ob_hi = place("ob_hi", [P, HEADS, S], F32R)
    half = HEADS // 2
    ob_lo = [place("ob_lo0", [P, half, S], F32R, at=cst_at), place("ob_lo1", [P, half, S], F32R)]
    assert cursor[0] <= nc.sbuf_usable_end
    y_hi = place("y_hi", [P, KT, S], F32R, at=base)
    y_lo = place("y_lo", [P, KT, S], F32R, at=base + KT * S * 4)
    th = place("th", [P, 2, S], at=tab_at)
    ysum = place("ysum", [P, 2, S], at=tab_at + 2 * S * 4)
    x_res = place("x_res", [P, NT, D], at=h_at)
    out_sb = place("out_sb", [P, NT, D], at=h_at + NT * D * 4)
    oscr = place("oscr", [P, NT, 2, S], at=par0 + HEADS * S * 4)
    w_ada_sb = place("w_ada_sb", [P, KT, 2 * D], at=base)
    x_sb = place("x_sb", [P, NT, D], at=base + KT * 2 * D * 4)
    scratch16 = place("scratch16", [P, 16, P], at=base + KT * 2 * D * 4)
    xT = place("xT", [P, KT, S], at=base + KT * 2 * D * 4 + NT * D * 4)
    rp = place("rp", [P, 4, 2 * S], at=w_lo_at)
    pos_i = place("pos_i", [P, S], I32, at=w_hi_at)
    pos_f = place("pos_f", [P, S], at=w_hi_at + S * 4)
    prow = place("prow", [P, P], at=w_hi_at + 2 * S * 4)
    prow2 = place("prow2", [3, P], at=w_hi_at + 2 * S * 4 + P * 4)
    cursor[0] = par0
    iq = place("iq", [P, 4, S])
    isw = place("isw", [P, 4, S])
    kpad = place("kpad", [P, 2, S])
    sm = place("sm", [P, NT, N_SMALL])
    cent = place("cent", [P, NT, IDX_DIM])
    csq = place("csq", [P, NT, IDX_DIM])
    assert cursor[0] <= zb_at
    cursor[0] = yy_at
    relu = place("relu", [P, 4, S])
    kx = place("kx", [P, S])
    ksw = place("ksw", [P, S])
    smT = place("smT", [P, S])
    assert cursor[0] <= after_solve
    kdup = place("kdup", [P, NT, P], at=wTn_at)
    bgate = place("bgate", [P, D], at=qk_at)
    pgain = place("pgain", [P, D], at=zraw_at)

    ps = ctx.enter_context(nc.psum_tensor("ps", [P, 8, S], F32))

    def bank(b):
        return ps[:, b, :]

    def tiles(ap):
        return ap.rearrange("p (i f) -> p i f", i=NT)

    ident, triu, ones = cst[:, C_ID, :], cst[:, C_TRIU, :], cst[:, C_ONES, :]

    def over_tiles(block):
        return cst[:, block:block + 1, :].to_broadcast([P, NT, P])

    G, GC, GL, BETA, EGC, EKD, EGL, BEGC, HBETA, TMP = range(10)

    def gh(slot, h, n=P):
        v = gsc[:, slot, :, bass.ds(h, 1)] if not isinstance(h, int) else gsc[:, slot, :, h:h + 1]
        return v.to_broadcast([P, NT, n]) if n > 1 else v

    def gcol(slot, h, i):
        return gsc[:, slot, i, bass.ds(h, 1)] if not isinstance(h, int) else gsc[:, slot, i, h:h + 1]

    def per_tile(ap, n=P):
        return ap.unsqueeze(2).to_broadcast([P, NT, n])

    def gflat(slot, h):
        return gh(slot, h, 1)

    def pcol_at(n, h):
        return pcol[:, 0, n + h:n + h + 1] if isinstance(h, int) else pcol[:, 0, bass.ds(h + n, 1)]

    def head_slot(buf, h):
        return buf[:, h, :]

    def blk(i):
        return slice(i * P, (i + 1) * P)

    def sem(name):
        return ctx.enter_context(nc.semaphore(name))

    def steps(name, names, ahead=0):
        return Steps(sem(name), names, ahead)

    s_rows, s_cst, s_pos, s_x, s_sc, s_bc, s_xres, s_out = (sem(n) for n in (
        "rows_loaded", "constants_loaded", "positions_loaded", "x_loaded", "scalars_loaded", "gate_rows_loaded",
        "residual_loaded", "output_stored"))
    s_ada = [sem(f"w_ada_loaded{k}") for k in range(KT)]
    s_raw = [sem(f"weights_loaded{s}") for s in range(RING)]
    hi_made, lo_made, unit_done = sem("hi_made"), sem("lo_made"), sem("unit_done")
    bank_free = [sem("proj_bank0_free"), sem("proj_bank1_free")]
    waits_passed = sem("waits_passed")
    LV = LEVELS[1:]

    pro_pe = steps("pro_pe", ["rowsT", "rows2T"] + [f"x{k}" for k in range(KT)] + ["mod"])
    pro_act = steps("pro_act", [f"ssq{i}" for i in range(NT)] + ["sinA", "sinI", "cos"] + [f"x{k}" for k in range(1, KT, 2)]
                    + [f"hi{k}" for k in range(KT)])
    pro_dve = steps("pro_dve", ["pcol", "pcol2", "cb", "hgain", "posf", "angA", "angI", "turns", "whole", "r1", "r2", "r3", "rc",
                                "wrap", "rc2", "clamp", "clampc"]
                    + [f"xn{i}" for i in range(NT)] + [f"x{k}" for k in range(0, KT, 2)]
                    + [f"m{b}" for b in range(16)] + ["mb", "scg", "h0"]
                    + [f"{a}{k - (a == 'lo')}" for k in range(1, KT) for a in ("h", "lo")] + [f"lo{KT - 1}"])
    pro_pool = steps("pro_pool", ["half", "eps_k", "eps_o", "ms", "rstd", "kpadE", "kpadO", "pad"])
    idx_pe = steps("idx_pe", ["smT", "kT", "gc", "gl"] + [f"gate{u}" for u in range(8)]
                   + [f"l{hd}_{qt}" for hd in range(8) for qt in (1, 2, 3)])
    idx_act = steps("idx_act", ["smT", "q0", "q1", "tanh", "ab", "na", "q2", "ln", "q3", "egc", "egl", "ekd"] + [f"gate{u}" for u in range(8)]
                    + [f"r{hd}_{qt}" for hd in range(8) for qt in (1, 2, 3)])
    idx_dve = steps("idx_dve", ["sm", "mu", "mus", "cent", "csq", "var", "iw", "z", "az", "kd0", "kd1", "beta", "sp1", "sp", "g"]
                    + [f"{a}{n}" for n in range(4) for a in ("sh", "ss")]
                    + ["kx", "ksh", "kss", "kcc", "kE", "kO", "gc", "dkd", "begc", "hbeta"] + [f"ad{n}" for n in range(4)]
                    + [f"s{hd}_{qt}" for hd in range(8) for qt in (1, 2, 3)]
                    + [f"{a}{qt}" for qt in (1, 2, 3) for a in ("tril", "fill")] + ["m0", "gb", "gp"])
    idx_pool = steps("idx_pool", ["ms", "rstd"] + [f"cc{n}" for n in range(4)])
    conv_act = steps("conv_act", ["raw_q", "tap_q", "raw_k", "tap_k", "tanh_q", "raw_v", "tap_v", "tanh_k", "tanh_v", "raw_z",
                            "tanh_z"])
    conv_dve = steps("conv_dve", ["q1", "q2", "q3", "qs", "k1", "k2", "k3", "ks", "v1", "v2", "v3", "vs", "zs"])
    top_dve = steps("top_dve", [f"{a}{t}{n}" for n in (0, 1) for t in (0, 1, 2) for a in ("max", "take")])
    solve_pe = steps("solve_pe", ["k", "q", "P", "v", "kn", "gram", "qk", "LT"]
                 + [f"{a}{s}" for s in LV for a in (("Z", "dU", "dT") if s < 64 else ("Z", "dU"))])
    solve_act = steps("solve_act", [f"k{i}" for i in range(NT)] + ["E"] + [f"q{i}" for i in range(NT)] + ["dec", "kT"])
    solve_dve = steps("solve_dve", ["kn", "y1", "yup", "ylo", "kbe", "kd", "vb", "L", "A", "T0", "T1", "U0", "U1"]
                  + [f"{a}{s}" for s in LV for a in (("Z", "U", "T") if s < 64 else ("Z", "U"))])
    solve_pool = steps("solve_pool", ["gbt", "msk", "rnk", "sbe", "skd", "mlow", "beta", "mup", "msq", "rnq", "qe"])
    scan_pe = steps("scan_pe", ["wT", "V0", "O0", "S0", "V1", "O1", "S1", "V2", "O2", "S2", "V3", "O3", "oT"], 1)
    scan_act = steps("scan_act", ["wTn", "o0", "o1", "o2", "o3", "so0", "so1", "so2", "so3"], 1)
    scan_dve = steps("scan_dve", ["vn0", "st0", "vn1", "st1", "vn2", "st2", "vn3", "on", "og"], 1)
    scan_pool = steps("scan_pool", ["r2", "ms", "ms2", "rs", "f"], 1)
    a_mask = steps("a_mask", ["m1", "m2", "m3"])
    a_act = steps("a_act", ["q", "k", "v", "z", "tanh"])
    rope_dve = steps("rope_dve", ["sh", "ss", "ad", "zs"])
    rope_pool = steps("rope_pool", ["cc"])
    attend_pe = steps("attend_pe", ["Vt", "s0", "s1", "s2", "s3", "pt0", "pt1", "pt2", "pt3", "pv"])
    attend_act = steps("attend_act", ["Vt", "e0", "e1", "e2", "e3", "pc0", "pc1", "pc2", "pc3"])
    attend_dve = steps("attend_dve", ["m0", "m1", "m2", "m3", "nb", "rc", "p0", "p1", "p2", "p3", "oa"])
    parts_act = steps("parts_act", ["ob_hi0", "ob_hi1", "oa_hi0", "oa_hi1"])
    parts_dve = steps("parts_dve", ["ob_lo0", "ob_lo1", "oa_lo0", "oa_lo1"])
    mix_act = steps("mix_act", ["ta", "tb", "yhi"])
    mix_dve = steps("mix_dve", ["yb", "ya", "ys", "ylo"])
    norm_pe = steps("norm_pe", [f"t{t}" for t in range(NT)])
    norm_act = steps("norm_act", [f"sq{t}" for t in range(NT)])
    norm_pool = steps("norm_pool", [f"{a}{t}" for t in range(NT) for a in ("ms", "rs")])
    norm_dve = steps("norm_dve", [f"{a}{t}" for t in range(NT) for a in ("n", "x")])

    def passed(eng):
        eng.sem_inc(waits_passed, 1)

    def q_of(it, j):
        return Q_LOOP + 4 * it + j

    def raw_value(slot, round_):
        return (round_ + 1) * 16 + (16 if slot == 0 else 0)


    block = ctx.enter_context(nc.Block())

    @block.sync
    def _(sp):
        sp.dma_start(prow[R_CONV:R_CONV + 96, :], conv_w.rearrange("w (m p) -> (w m) p", p=P)).then_inc(s_rows, 16)
        sp.dma_start(prow[R_GAIN:R_GAIN + 8, :], pre_gain.rearrange("(m p) -> m p", p=P)).then_inc(s_rows, 16)
        sp.dma_start(prow[R_BADA:R_BADA + 16, :], b_ada[0:2 * D].rearrange("(m p) -> m p", p=P)).then_inc(s_rows, 16)
        sp.dma_start(prow[R_C:R_C + 8, :], c.rearrange("a (m p) -> (a m) p", p=P)).then_inc(s_rows, 16)
        for r, v in ((R2_LNG, ln_gain), (R2_LNB, ln_bias)):
            for n in range(2):
                sp.dma_start(prow2[r:r + 1, n * IDX_DIM:(n + 1) * IDX_DIM],
                             v.rearrange("(a n) -> a n", a=1)).then_inc(s_rows, 16)
        sp.dma_start(prow2[R2_NG:R2_NG + 1, :], norm_gain.rearrange("(a n) -> a n", a=1)).then_inc(s_rows, 16)
        sp.dma_start(cst[:], cst_in).then_inc(s_cst, 16)
        sp.dma_start(cols[:], cols_in).then_inc(s_cst, 16)
        sp.dma_start(x_sb[:], x.rearrange("(i p) d -> p i d", p=P)).then_inc(s_x, 16)
        sp.dma_start(pos_i[:], positions.to_broadcast([P, S])).then_inc(s_pos, 16)
        sp.dma_start(small_cols[:, 48:56], a_log.rearrange("(a n) -> a n", a=1).to_broadcast([P, 8])).then_inc(s_sc, 16)
        sp.dma_start(small_cols[:, 56:64], dt_bias.rearrange("(a n) -> a n", a=1).to_broadcast([P, 8])).then_inc(s_sc, 16)
        for k in range(KT):
            sp.dma_start(w_ada_sb[:, k, :], w_ada[k * P:(k + 1) * P, 0:2 * D]).then_inc(s_ada[k], 16)

        def columns(w, col):
            return w.rearrange("(k p) n -> p k n", p=P)[:, :, bass.ds(col, P)]

        wv = w_in.rearrange("(k p) n -> p k n", p=P)
        n_ik = IDX_DIM + IDX_HEADS
        sp.dma_start(raw[:, 0, :, 0:n_ik], wv[:, :, COL_IK:COL_IK + n_ik]).then_inc(s_raw[0], 16)
        sp.dma_start(raw[:, 0, :, n_ik:N_SMALL], wv[:, :, COL_BETA:COL_BETA + 2 * HEADS]).then_inc(s_raw[0], 16)
        for u in range(1, U_LOOP):
            if u >= RING:
                if u - RING < U_GATE:
                    sp.wait_ge(hi_made, u - RING + 1)
                    sp.wait_ge(lo_made, u - RING + 1)
                else:
                    sp.wait_ge(*idx_pe.at(f"gate{u - RING - U_GATE}"))
            src = columns(w_in, COL_IQ + (u - U_IQ) * P) if u < U_GATE else columns(w_ada, 2 * D + (u - U_GATE) * P)
            sp.dma_start(raw[:, u % RING, :, :], src).then_inc(s_raw[u % RING], 16)
            if u == U_GATE:
                sp.wait_ge(*pro_dve.at("lo7"))
                sp.dma_start(bgate[:], b_ada[2 * D:3 * D].rearrange("(a n) -> a n", a=1).to_broadcast([P, D])).then_inc(s_bc, 16)
                sp.dma_start(pgain[:], post_gain.rearrange("(a n) -> a n", a=1).to_broadcast([P, D])).then_inc(s_bc, 16)

        def load(it, j, src):
            slot = (1 + j) % RING
            if isinstance(it, int) and it == 0:
                sp.wait_ge(*idx_pe.at(f"gate{4 + j}"))
            else:
                sp.wait_ge(lo_made, q_of(it, j) - RING + 1)
                passed(sp)
            sp.dma_start(raw[:, slot, :, :], src).then_inc(s_raw[slot], 16)

        for j, col in enumerate((COL_BQ, COL_BK, COL_BV, COL_BZ)):
            load(0, j, columns(w_in, col))
        with sp.Fori(1, HEADS) as h:
            for j, col in enumerate((COL_BQ, COL_BK, COL_BV, COL_BZ)):
                load(h, j, columns(w_in, col + h * P))
        with sp.Fori(0, HEADS) as h:
            for j, col in enumerate((COL_AQ, COL_AK, COL_AV, COL_AZ)):
                load(h + HEADS, j, columns(w_in, col + h * P))
        with sp.Fori(0, KT) as m:
            for j, (w, col) in enumerate(((w_in, COL_GA), (w_in, COL_GB), (w_b_out, 0), (w_a_out, 0))):
                load(m + 2 * HEADS, j, columns(w, col + m * P))
        for n, col in enumerate(OUT_COLS):
            load(ITERS + n // 4, n % 4, columns(w_o, col))
        sp.wait_ge(unit_done, q_of(ITERS - 1, 1) + 1)
        sp.dma_start(x_res[:], x.rearrange("(i p) d -> p i d", p=P)).then_inc(s_xres, 16)
        for t in range(NT):
            sp.wait_ge(*norm_dve.at(f"x{t}"))
            sp.dma_start(out[t * P:(t + 1) * P, :], out_sb[:, t, :]).then_inc(s_out, 16)
        sp.wait_ge(s_out, 16 * NT)

    @block.tensor
    def _(pe):
        scan_pe.count_ahead(pe)

        def group(out_ap, terms):
            for n, (a, b) in enumerate(terms):
                mm = pe.matmul(out_ap, a, b, start=(n == 0), stop=(n == len(terms) - 1))
            return mm

        def project(q, slot, rhs_hi, rhs_lo, ks, m=P, bank_no=None, first_uses=0):
            out_ap = ps[0:m, bank_no, :]
            for k in ks:
                if k == 0:
                    pe.wait_ge(hi_made, q + 1)
                    pe.wait_ge(lo_made, q + 1)
                pe.matmul(out_ap, w_hi[:, slot, k, 0:m], rhs_hi(k), start=(k == 0), stop=False)
                pe.matmul(out_ap, w_hi[:, slot, k, 0:m], rhs_lo(k), start=False, stop=False)
                mm = pe.matmul(out_ap, w_lo[:, slot, k, 0:m], rhs_hi(k), start=False, stop=(k == KT - 1))
                if k == KT - 1:
                    mm.then_inc(unit_done, 1)

        def h_rhs(k):
            return h_hi[:, k, :]

        def hl_rhs(k):
            return h_lo[:, k, :]

        def ob_lo_rhs(k):
            return ob_lo[k // half][:, k % half, :]

        def part(it, rnd, rhs=(h_rhs, hl_rhs)):
            j, ks = rnd // 4, range(2 * (rnd % 4), 2 * (rnd % 4) + 2)
            b = (1 + j) % 2
            if rnd % 4 == 0:
                pe.wait_ge(bank_free[b], 2 * it + (Q_LOOP + j) // 2)
            project(q_of(it, j), (1 + j) % RING, rhs[0], rhs[1], ks, bank_no=b)

        EARLY = 4
        pe.wait_ge(s_rows, 16 * 9)
        pe.wait_ge(s_cst, 32)
        pe.transpose(ps[:, 2, 0:P], prow[:], ident).then_inc(*pro_pe.inc("rowsT"))
        pe.transpose(ps[:, 2, P:P + 3], prow2[:], ident[0:3, 0:3]).then_inc(*pro_pe.inc("rows2T"))
        def condition(ks):
            for k in ks:
                pe.wait_ge(s_ada[k], 16)
                for n in range(4):
                    mm = pe.matmul(bank(2 + n), cb[:, k, :], w_ada_sb[:, k, n * S:(n + 1) * S], start=(k == 0),
                                   stop=(k == KT - 1))
            return mm

        pe.wait_ge(*pro_dve.at("cb"))
        pe.wait_ge(*pro_dve.at("pcol2"))
        condition(range(EARLY))
        XB = [0, 1, 6, 7]
        for k in range(KT):
            if k == 0:
                pe.wait_ge(*pro_dve.at(f"xn{NT - 1}"))
            if k >= 4:
                pe.wait_ge(*(pro_dve if k % 2 == 0 else pro_act).at(f"x{k - 4}"))
            for i in range(NT):
                mm = pe.transpose(ps[:, XB[k % 4], blk(i)], x_sb[:, i, blk(k)], ident)
            mm.then_inc(*pro_pe.inc(f"x{k}"))
        condition(range(EARLY, KT)).then_inc(*pro_pe.inc("mod"))

        def whole(q, m=P):
            if q >= 2:
                pe.wait_ge(bank_free[q % 2], q // 2)
            project(q, q % RING, h_rhs, hl_rhs, range(KT), m, q % 2)

        for k in range(KT):
            pe.wait_ge(*pro_act.at(f"hi{k}"))
            pe.wait_ge(*pro_dve.at(f"lo{k}"))
            project(0, 0, h_rhs, hl_rhs, [k], N_SMALL, 0)
            project(1, 1, h_rhs, hl_rhs, [k], P, 1)
        pe.wait_ge(*idx_act.at("smT"))
        for i in range(NT):
            mm = pe.transpose(ps[:, 2, i * P:i * P + N_SMALL], smT[0:N_SMALL, blk(i)], ident[0:N_SMALL, 0:N_SMALL])
        mm.then_inc(*idx_pe.inc("smT"))
        for q in range(2, 5):
            whole(q)
        pe.wait_ge(*idx_dve.at("kd1"))
        for i in range(NT):
            mm = pe.transpose(ps[:, 3, blk(i)], kdup[:, i, :], ident)
        mm.then_inc(*idx_pe.inc("kT"))
        pe.wait_ge(*idx_dve.at("g"))
        g_all = gsc[:, G, :, :].rearrange("p i h -> p (i h)")
        pe.matmul(ps[:, 4, 0:NT * HEADS], triu, g_all, start=True, stop=True).then_inc(*idx_pe.inc("gc"))
        pe.matmul(ps[:, 4, NT * HEADS:2 * NT * HEADS], ones, g_all, start=True, stop=True).then_inc(*idx_pe.inc("gl"))
        for n in range(8):
            u = U_GATE + n
            pe.wait_ge(s_raw[u % RING], raw_value(u % RING, u // RING))
            if n >= 2:
                pe.wait_ge(*idx_act.at(f"gate{n - 2}"))
            group(ps[:, 6 + n % 2, 0:P], [(cb[:, k, :], raw[:, u % RING, k, :]) for k in range(KT)]).then_inc(
                *idx_pe.inc(f"gate{n}"))
        pe.wait_ge(*idx_dve.at("kO"))
        pe.wait_ge(*idx_dve.at("gc"))
        order = [(hd, qt) for hd in range(8) for qt in (1, 2, 3)]
        for m, (hd, qt) in enumerate(order):
            if qt == 1:
                pe.wait_ge(*idx_dve.at(f"ad{hd // 2}"))
            if m >= 4:
                pe.wait_ge(*idx_act.at("r{}_{}".format(*order[m - 4])))
            n = (qt + 1) * P
            pe.matmul(ps[:, 2 + m % 4, 0:n], iq[:, hd // 2, blk(qt)], kpad[:, hd % 2, 0:n], start=True,
                      stop=True).then_inc(*idx_pe.inc(f"l{hd}_{qt}"))

        def prepare(h, rnd):
            if rnd == 15:
                if before_first(h - 1):
                    pe.wait_ge(*idx_act.at("r7_3"))
                else:
                    pe.wait_ge(*solve_dve.at("T32", h - 1))
                for name, b, y in (("k", 5, 1), ("q", 4, 0)):
                    pe.wait_ge(*conv_dve.at(name + "s", h))
                    for i in range(NT):
                        mm = pe.transpose(ps[:, b, blk(i)], y3[:, y, blk(i)], ident)
                    mm.then_inc(*solve_pe.inc(name))

        def solve(h, par, rnd):
            if rnd == 0:
                pe.wait_ge(*solve_pool.at("gbt", h))
                for i in range(NT):
                    mm = pe.matmul(ps[:, 2, blk(i)], L[:, i, :], triu, start=True, stop=True)
                mm.then_inc(*solve_pe.inc("P"))
            elif rnd == 1:
                pe.wait_ge(*conv_dve.at("vs", h))
                if not before_first(h - 1):
                    pe.wait_ge(*solve_dve.at("U64", h - 1))
                for i in range(NT):
                    mm = pe.transpose(ps[:, 3, blk(i)], y3[:, 2, blk(i)], ident)
                mm.then_inc(*solve_pe.inc("v"))
                pe.wait_ge(*solve_dve.at("y1", h))
                pe.wait_ge(*solve_act.at("E", h))
                for i in range(NT):
                    mm = pe.transpose(ps[:, 2, blk(i)], kn[:, i, :], ident)
                mm.then_inc(*solve_pe.inc("kn"))
            elif rnd == 2:
                pe.wait_ge(*solve_act.at("kT", h))
                pe.wait_ge(*solve_dve.at("kd", h))
                for i in range(NT):
                    mm = pe.matmul(ps[:, 5, blk(i)], kT[:, blk(i)], kT[:, blk(i)], start=True, stop=True)
                mm.then_inc(*solve_pe.inc("gram"))
                for i in range(NT):
                    mm = pe.matmul(ps[:, 4, blk(i)], kT[:, blk(i)], y3[:, 0, blk(i)], start=True, stop=True)
                mm.then_inc(*solve_pe.inc("qk"))
            elif rnd == 3:
                pe.wait_ge(*solve_dve.at("L", h))
                pe.wait_ge(*solve_dve.at("vb", h))
                for i in range(NT):
                    mm = pe.transpose(ps[:, 3, blk(i)], L[:, i, :], ident)
                mm.then_inc(*solve_pe.inc("LT"))
            elif rnd % 2 == 0:
                s = LEVELS[rnd // 2 - 1]
                if s == 2:
                    pe.wait_ge(*solve_dve.at("A", h))
                    pe.wait_ge(*solve_dve.at("U1", h))
                else:
                    pe.wait_ge(*solve_dve.at(f"U{s // 2}", h))
                for i in range(NT):
                    mm = pe.matmul(ps[:, 2, blk(i)], L[:, i, :], U[:, par, i, :], start=True, stop=True)
                mm.then_inc(*solve_pe.inc(f"Z{s}"))
            if rnd % 2 == 1 and rnd >= 5:
                s = LEVELS[rnd // 2 - 1]
                pe.wait_ge(*solve_dve.at(f"Z{s}", h))
                pe.wait_ge(*solve_dve.at("T1" if s == 2 else f"T{s // 2}", h))
                for i in range(NT):
                    mm = pe.matmul(ps[:, 3, blk(i)], T[:, i, :], kn[:, i, :], start=True, stop=True)
                mm.then_inc(*solve_pe.inc(f"dU{s}"))
                if s < 64:
                    for i in range(NT):
                        mm = pe.matmul(ps[:, 4, blk(i)], kn[:, i, :], T[:, i, :], start=True, stop=True)
                    mm.then_inc(*solve_pe.inc(f"dT{s}"))

        def scan(h, par, rnd):
            if rnd == 0:
                pe.wait_ge(*solve_dve.at("U64", h))
                pe.wait_ge(*solve_dve.at("kbe", h))
                if before_first(h - 1):
                    pe.wait_ge(*idx_act.at("gate7"))
                else:
                    if not before_first(h - 1):
                        pe.wait_ge(*scan_dve.at("og", h - 1))
                for i in range(NT):
                    mm = pe.matmul(ps[:, 7, blk(i)], kbe[:, par, i, :], U[:, par, i, :], start=True, stop=True)
                mm.then_inc(*scan_pe.inc("wT"))
            elif 1 <= rnd <= 8 and rnd % 2 == 1:
                i = rnd // 2
                if i == 0:
                    if not before_first(h - 1):
                        pe.wait_ge(*scan_act.at("o3", h - 1))
                else:
                    pe.wait_ge(*scan_act.at(f"o{i - 1}", h))
                    pe.wait_ge(*scan_dve.at(f"st{i - 1}", h))
                mm = pe.matmul(ps[:, 6, 0:P], U[:, par, i, :], vb[:, par, i, :], start=True, stop=(i == 0))
                if i > 0:
                    if i == 1:
                        pe.wait_ge(*scan_act.at("wTn", h))
                    mm = pe.matmul(ps[:, 6, 0:P], wTn[:, blk(i)], state[:], start=False, stop=True)
                mm.then_inc(*scan_pe.inc(f"V{i}"))
            elif 1 <= rnd <= 8:
                i = rnd // 2 - 1
                pe.wait_ge(*scan_dve.at(f"vn{i}", h))
                if i == 0:
                    pe.wait_ge(*solve_pool.at("qe", h))
                    pe.wait_ge(*scan_act.at("wTn", h))
                if i > 0:
                    pe.matmul(ps[:, 6, P:2 * P], qe[:, par, blk(i)], state[:], start=True, stop=False)
                pe.matmul(ps[:, 6, P:2 * P], intra[:, par, i, :], vnew[:], start=(i == 0), stop=True).then_inc(
                    *scan_pe.inc(f"O{i}"))
                if i < NT - 1:
                    pe.matmul(ps[:, 7, 0:P], kd[:, par, i, :], vnew[:], start=True, stop=True).then_inc(
                        *scan_pe.inc(f"S{i}"))
            elif rnd == 12:
                pe.wait_ge(*scan_dve.at("on", h))
                for i in range(NT):
                    mm = pe.transpose(ps[:, 7, blk(i)], o_tok[:, i, :], ident)
                mm.then_inc(*scan_pe.inc("oT"))

        def attend(h, rnd):
            if rnd == 0:
                pe.wait_ge(*a_act.at("v", h))
                if not before_first(h - 1):
                    pe.wait_ge(*attend_dve.at("oa", h - 1))
                for i in range(NT):
                    mm = pe.transpose(ps[:, 2, blk(i)], vT[:, blk(i)], ident)
                mm.then_inc(*attend_pe.inc("Vt"))
            elif rnd in (1, 2):
                if rnd == 1:
                    pe.wait_ge(*rope_dve.at("ad", h))
                    if not before_first(h - 1):
                        pe.wait_ge(*attend_act.at("pc3", h - 1))
                for qt in (0, 1) if rnd == 1 else (2, 3):
                    if qt == 3:
                        pe.wait_ge(*attend_act.at("Vt", h))
                    n = (qt + 1) * P
                    pe.matmul(ps[:, (3, 4, 5, 2)[qt], 0:n], qk[:, 0, blk(qt)], qk[:, 1, 0:n], start=True,
                              stop=True).then_inc(*attend_pe.inc(f"s{qt}"))
            elif rnd in (5, 6):
                for kt in (0, 1) if rnd == 5 else (2, 3):
                    for qt in range(kt, NT):
                        if kt == 0:
                            pe.wait_ge(*attend_dve.at(f"p{qt}", h))
                        mm = pe.transpose(ps[:, (3, 4, 5, 2)[kt], blk(qt)], prob[:, qt, blk(kt)], ident)
                    mm.then_inc(*attend_pe.inc(f"pt{kt}"))
            elif rnd == 8:
                for kt in range(NT):
                    pe.wait_ge(*attend_act.at(f"pc{kt}", h))
                    mm = pe.matmul(ps[:, 3, kt * P:S], Vt[:, kt, :], probT[:, kt, kt * P:S], start=(kt == 0),
                                   stop=(kt == NT - 1), skip_group_check=True)
                mm.then_inc(*attend_pe.inc("pv"))

        for rnd in range(ROUNDS):
            prepare(0, rnd)
            part(0, rnd)
        for rnd in range(ROUNDS):
            solve(0, 0, rnd)
            prepare(1, rnd)
            part(1, rnd)
        with pe.Fori(0, 3) as pair:
            for par in range(2):
                h = pair * 2 + (2 + par)
                for rnd in range(ROUNDS):
                    solve(h - 1, 1 - par, rnd)
                    prepare(h, rnd)
                    scan(h - 2, par, rnd)
                    part(h, rnd)
        for rnd in range(ROUNDS):
            solve(7, 1, rnd)
            scan(6, 0, rnd)
            part(8, rnd)
        for rnd in range(ROUNDS):
            scan(7, 1, rnd)
            attend(0, rnd)
            part(9, rnd)
        with pe.Fori(2, HEADS) as h:
            for rnd in range(ROUNDS):
                attend(h - 1, rnd)
                part(h + 8, rnd)

        def mixed_part(it, rnd):
            j = rnd // 4
            if j >= 2 and rnd % 2 == 0 and isinstance(it, int):
                name, n = ("ob", "oa")[j - 2], rnd % 4 // 2
                pe.wait_ge(*parts_dve.at(f"{name}_lo{n}"))
            part(it, rnd, ((h_rhs, hl_rhs), (h_rhs, hl_rhs), (lambda k: ob_hi[:, k, :], ob_lo_rhs),
                           (lambda k: oa_hi[:, k, :], lambda k: oa_lo[:, k, :]))[j])

        for rnd in range(ROUNDS):
            if rnd < 10:
                attend(7, rnd)
            mixed_part(16, rnd)
        with pe.Fori(1, KT) as m:
            for rnd in range(ROUNDS):
                mixed_part(m + 16, rnd)

        pe.wait_ge(*mix_act.at("yhi", KT - 2))
        pe.wait_ge(*mix_dve.at("ylo", KT - 2))
        for g in range(4):
            slots = slice(1, 3) if g % 2 == 0 else slice(0, 4, 3)
            pe.wait_ge(hi_made, Q_OUT + 2 * g + 2)
            pe.wait_ge(lo_made, Q_OUT + 2 * g + 2)
            if g == 0:
                order = ([(t, k) for t in (1, 2, 3) for k in range(KT - 1)] + [(t, KT - 1) for t in (1, 2, 3)]
                         + [(0, k) for k in range(KT)])
            else:
                order = [(t, k) for t in range(NT) for k in range(KT)]
            for t, k in order:
                if g == 0 and (t, k) == (1, KT - 1):
                    pe.wait_ge(*mix_act.at("yhi", KT - 1))
                    pe.wait_ge(*mix_dve.at("ylo", KT - 1))
                if g == 0 and (t, k) == (0, 0):
                    pe.wait_ge(bank_free[0], (Q_OUT + 1) // 2)
                    pe.wait_ge(bank_free[1], Q_OUT // 2)
                o_ap = ps[:, 2 * t + g // 2, (g % 2) * 256:(g % 2) * 256 + 256]
                pe.matmul(o_ap, y_hi[:, k, blk(t)], w_hi[:, slots, k, :], start=(k == 0), stop=False)
                pe.matmul(o_ap, y_hi[:, k, blk(t)], w_lo[:, slots, k, :], start=False, stop=False)
                mm = pe.matmul(o_ap, y_lo[:, k, blk(t)], w_hi[:, slots, k, :], start=False, stop=(k == KT - 1))
                if g == 3 and k == KT - 1:
                    mm.then_inc(*norm_pe.inc(f"t{t}"))
            if g < 3:
                mm.then_inc(unit_done, 2)

    @block.scalar
    def _(act):
        scan_act.count_ahead(act)

        def split(q, slot, raw_at, n=P):
            act.wait_ge(s_raw[slot], raw_at)
            if isinstance(q, int) and q < RING:
                if q == 0:
                    act.wait_ge(*pro_act.at("cos"))
                    act.wait_ge(*pro_act.at("sinI"))
            else:
                act.wait_ge(unit_done, q - RING + 1)
            act.activation(w_hi[:, slot, :, 0:n], raw[:, slot, :, 0:n], ACT.Copy).then_inc(hi_made, 1)

        def split_ahead(it, rnd):
            if rnd % 4 == 1:
                j = rnd // 4 + 2
                slot = (1 + j) % RING
                split(q_of(it, j), slot, (it + (3 + (1 + j) // RING) + 1) * 16 + (16 if slot == 0 else 0))

        def arrived(it, j):
            act.wait_ge(unit_done, q_of(it, j) + 1)

        def proj_bank(j):
            return (1 + j) % 2

        act.wait_ge(s_x, 16)
        for i in range(NT):
            if i > 0:
                act.wait_ge(*pro_act.at(f"ssq{i - 1}"))
            act.activation(xT[:, 0:2, :], x_sb[:, i, :].rearrange("p (a b) -> p a b", a=2), ACT.Square,
                           accum_out=small_cols[:, i:i + 1]).then_inc(*pro_act.inc(f"ssq{i}"))
        act.wait_ge(s_cst, 32)
        act.wait_ge(*pro_dve.at("clampc"))
        for t, name in ((0, "sinA"), (1, "sinI")):
            act.activation(tab_sin[:, t, :], rp[:, 2, t * S:(t + 1) * S], ACT.Sin, scale=cols[:, 2 + t:3 + t]).then_inc(
                *pro_act.inc(name))
        act.activation(tab_cos[:].rearrange("p a b -> p (a b)"), rp[:, 3, :], ACT.Sin).then_inc(*pro_act.inc("cos"))
        for k in range(1, KT, 2):
            act.wait_ge(*pro_pe.at(f"x{k}"))
            act.activation(xT[:, k, :], ps[:, [0, 1, 6, 7][k % 4], :], ACT.Copy).then_inc(*pro_act.inc(f"x{k}"))
        split(0, 0, raw_value(0, 0), N_SMALL)
        split(1, 1, raw_value(1, 0))
        for k in range(KT):
            act.wait_ge(*pro_dve.at(f"h{k}"))
            act.activation(h_hi[:, k, :], xT[:, k, :], ACT.Copy).then_inc(*pro_act.inc(f"hi{k}"))

        def take(q, out_ap, step, m=P):
            act.wait_ge(unit_done, q + 1)
            act.activation(out_ap, ps[0:m, q % 2, :], ACT.Copy).then_inc(*idx_act.inc(step))

        def freed(q, step):
            act.wait_ge(*idx_act.at(step))
            act.sem_inc(bank_free[q % 2], 1)

        take(0, smT[0:N_SMALL, :], "smT", N_SMALL)
        freed(0, "smT")
        split(2, 2, raw_value(2, 0))
        take(1, iq[:, 0, :], "q0")
        freed(1, "q0")
        split(3, 3, raw_value(3, 0))
        take(2, iq[:, 1, :], "q1")
        freed(2, "q1")
        split(4, 0, raw_value(0, 1))
        act.wait_ge(*idx_dve.at("sm"))
        act.activation(gsc[:, TMP, :, :], sm[:, :, SM_BETA:SM_BETA + HEADS], ACT.Tanh, scale=0.5).then_inc(*idx_act.inc("tanh"))
        act.wait_ge(*idx_dve.at("az"))
        act.activation(gsc[:, EGC, :, :], gsc[:, EKD, :, :], ACT.Exp, scale=-1.0).then_inc(*idx_act.inc("ab"))
        act.wait_ge(s_sc, 32)
        act.activation(small_cols[:, 48:56], small_cols[:, 48:56], ACT.Exp).then_inc(*idx_act.inc("na"))
        take(3, iq[:, 2, :], "q2")
        freed(3, "q2")
        act.wait_ge(*idx_dve.at("sp1"))
        act.activation(gsc[:, EGC, :, :], gsc[:, EGC, :, :], ACT.Ln).then_inc(*idx_act.inc("ln"))
        take(4, iq[:, 3, :], "q3")
        freed(4, "q3")
        act.wait_ge(*idx_dve.at("dkd"))
        act.activation(gsc[:, EGC, :, :], gsc[:, GC, :, :], ACT.Exp).then_inc(*idx_act.inc("egc"))
        act.activation(gsc[:, EGL, :, :], gsc[:, GL, :, :], ACT.Exp).then_inc(*idx_act.inc("egl"))
        act.activation(gsc[:, EKD, :, :], gsc[:, TMP, :, :], ACT.Exp).then_inc(*idx_act.inc("ekd"))
        for n in range(8):
            act.wait_ge(*idx_pe.at(f"gate{n}"))
            act.activation(gate[:, blk(n)], ps[:, 6 + n % 2, 0:P], ACT.Copy).then_inc(*idx_act.inc(f"gate{n}"))
        split(5, 1, raw_value(1, 3))
        split(6, 2, raw_value(2, 3))
        order = [(hd, qt) for hd in range(8) for qt in (1, 2, 3)]
        for m, (hd, qt) in enumerate(order):
            act.wait_ge(*idx_pe.at(f"l{hd}_{qt}"))
            if m >= 4:
                act.wait_ge(*idx_dve.at("s{}_{}".format(*order[m - 4])))
            n = (qt + 1) * P
            act.activation(relu[:, m % 4, 0:n], ps[:, 2 + m % 4, 0:n], ACT.Relu, scale=IDX_DIM ** -0.5).then_inc(
                *idx_act.inc(f"r{hd}_{qt}"))

        def unit(h, j, name):
            b = proj_bank(j)
            arrived(h, j)
            if name == "z":
                if not before_first(h - 1):
                    act.wait_ge(*conv_dve.at("zs", h - 1))
                act.activation(zraw[:], bank(b), ACT.Copy).then_inc(*conv_act.inc("raw_z"))
                act.wait_ge(*conv_act.at("raw_z", h))
            else:
                if not before_first(h - 1):
                    act.wait_ge(*conv_dve.at(name + "3", h - 1))
                act.activation(rows[:, j, 3:3 + S], bank(b), ACT.Copy).then_inc(*conv_act.inc(f"raw_{name}"))
                if not before_first(h - 1):
                    act.wait_ge(*solve_pe.at(name, h - 1))
                if name == "q":
                    if not before_first(h - 1):
                        act.wait_ge(*solve_pe.at("qk", h - 1))
                    if not before_first(h - 1):
                        act.wait_ge(*solve_pool.at("qe", h - 1))
                w = R_CONV + 3 * 24 + j * 8
                act.activation(y3[:, j, :], bank(b), ACT.Copy, scale=pcol_at(w, h)).then_inc(
                    *conv_act.inc(f"tap_{name}"))
                act.wait_ge(*conv_act.at(f"tap_{name}", h))
            act.sem_inc(bank_free[b], 1)

        def delta_rows(h, par, rnd):
            def tanh(name, j):
                act.wait_ge(*conv_dve.at(name + "3", h))
                if not before_first(h if name != "q" else h - 1):
                    act.wait_ge(*conv_dve.at("zs" if name == "q" else {"k": "qs", "v": "ks"}[name], h if name != "q" else h - 1))
                act.activation(tz[:], y3[:, j, :], ACT.Tanh, scale=0.5).then_inc(*conv_act.inc(f"tanh_{name}"))

            if isinstance(h, int) and h == 0 and rnd == 4:
                act.wait_ge(*idx_dve.at("gp"))
            if rnd == 4:
                unit(h, 0, "q")
            elif rnd == 8:
                unit(h, 1, "k")
                tanh("q", 0)
            elif rnd == 12:
                unit(h, 2, "v")
                tanh("k", 1)
            elif rnd == 15:
                tanh("v", 2)
                act.wait_ge(*solve_pe.at("k", h))
                if not before_first(h - 2):
                    act.wait_ge(*scan_pool.at("f", h - 2))
                for i in range(NT):
                    act.activation(junk[:, blk(i)], ps[:, 5, blk(i)], ACT.Square,
                                   accum_out=st8[:, par, i:i + 1]).then_inc(*solve_act.inc(f"k{i}"))

        def delta_z(h, rnd):
            if rnd == 1:
                unit(h, 3, "z")
                act.wait_ge(*conv_dve.at("vs", h))
                act.activation(tz[:], zraw[:], ACT.Tanh, scale=0.5).then_inc(*conv_act.inc("tanh_z"))

        def solve(h, par, rnd):
            if rnd == 0:
                act.wait_ge(*solve_pe.at("P", h))
                if not before_first(h - 1):
                    act.wait_ge(*solve_pool.at("qe", h - 1))
                act.activation(E[:], bank(2), ACT.Exp).then_inc(*solve_act.inc("E"))
                for i in range(NT):
                    act.activation(junk[:, (4 + i) * P:(5 + i) * P], ps[:, 4, blk(i)], ACT.Square,
                                   accum_out=st8[:, par, 4 + i:5 + i]).then_inc(*solve_act.inc(f"q{i}"))
                act.wait_ge(*solve_dve.at("ylo", h))
                act.activation(yy[:], yy[:], ACT.Exp).then_inc(*solve_act.inc("dec"))
            elif rnd == 1:
                act.wait_ge(*solve_pe.at("kn", h))
                act.activation(kT[:], bank(2), ACT.Copy).then_inc(*solve_act.inc("kT"))

        def scan(h, par, rnd):
            if rnd == 0:
                act.wait_ge(*scan_pe.at("wT", h))
                if not before_first(h - 1):
                    act.wait_ge(*scan_pe.at("V3", h - 1))
                act.activation(wTn[:], bank(7), ACT.Copy, scale=-1.0).then_inc(*scan_act.inc("wTn"))
            elif 1 <= rnd <= 8 and rnd % 2 == 0:
                i = rnd // 2 - 1
                act.wait_ge(*scan_pe.at(f"O{i}", h))
                if i == 0:
                    if not before_first(h - 1):
                        act.wait_ge(*scan_pe.at("oT", h - 1))
                act.activation(o_tok[:, i, :], ps[:, 6, P:2 * P], ACT.Copy).then_inc(*scan_act.inc(f"o{i}"))
            elif rnd == 9:
                act.wait_ge(*scan_act.at("o3", h))
                if not before_first(h - 1):
                    act.wait_ge(*scan_pool.at("f", h - 1))
                for i in range(NT):
                    act.activation(junk[:, (8 + i) * P:(9 + i) * P], o_tok[:, i, :], ACT.Square,
                                   accum_out=fo[:, 0, i:i + 1]).then_inc(*scan_act.inc(f"so{i}"))

        def attention_rows(h, rnd):
            targets = {4: (0, "q", qk[:, 0, :]), 8: (1, "k", qk[:, 1, :]), 12: (2, "v", vT[:]), 15: (3, "z", zraw[:])}
            if rnd in targets:
                j, name, dst = targets[rnd]
                arrived(h + 8, j)
                if name in "qk":
                    if not before_first(h - 1):
                        act.wait_ge(*attend_pe.at("s3", h - 1))
                elif name == "v":
                    if not before_first(h - 1):
                        act.wait_ge(*attend_pe.at("Vt", h - 1))
                elif isinstance(h, int) and h == 0:
                    act.wait_ge(*conv_dve.at("zs", HEADS - 1))
                else:
                    if not before_first(h - 1):
                        act.wait_ge(*rope_dve.at("zs", h - 1))
                act.activation(dst, bank(proj_bank(j)), ACT.Copy).then_inc(*a_act.inc(name))
                act.wait_ge(*a_act.at(name, h))
                act.sem_inc(bank_free[proj_bank(j)], 1)
            if rnd == 15:
                if not before_first(h - 1):
                    act.wait_ge(*attend_dve.at("oa", h - 1))
                act.activation(tz[:], zraw[:], ACT.Tanh, scale=0.5).then_inc(*a_act.inc("tanh"))

        def attend(h, rnd):
            if rnd == 0:
                act.wait_ge(*attend_pe.at("Vt", h))
                act.activation(Vt[:].rearrange("p i f -> p (i f)"), bank(2), ACT.Copy).then_inc(*attend_act.inc("Vt"))
            elif rnd == 3:
                act.wait_ge(*attend_dve.at("nb", h))
                for qt in range(NT):
                    n = (qt + 1) * P
                    act.activation(prob[:, qt, 0:n], prob[:, qt, 0:n], ACT.Exp, bias=amx[:, 1, qt:qt + 1],
                                   scale=HD ** -0.5, accum_out=amx[:, 2, qt:qt + 1]).then_inc(*attend_act.inc(f"e{qt}"))
            elif rnd in (6, 7):
                for kt in (0, 1) if rnd == 6 else (2, 3):
                    act.wait_ge(*attend_pe.at(f"pt{kt}", h))
                    act.activation(probT[:, kt, kt * P:S], ps[:, (3, 4, 5, 2)[kt], kt * P:S], ACT.Copy).then_inc(
                        *attend_act.inc(f"pc{kt}"))

        for rnd in range(ROUNDS):
            delta_rows(0, 0, rnd)
            split_ahead(0, rnd)
        for rnd in range(ROUNDS):
            solve(0, 0, rnd)
            delta_z(0, rnd)
            delta_rows(1, 1, rnd)
            split_ahead(1, rnd)
        with act.Fori(0, 3) as pair:
            for par in range(2):
                h = pair * 2 + (2 + par)
                for rnd in range(ROUNDS):
                    solve(h - 1, 1 - par, rnd)
                    scan(h - 2, par, rnd)
                    delta_z(h - 1, rnd)
                    delta_rows(h, par, rnd)
                    split_ahead(h, rnd)
        for rnd in range(ROUNDS):
            solve(7, 1, rnd)
            scan(6, 0, rnd)
            delta_z(7, rnd)
            attention_rows(0, rnd)
            split_ahead(8, rnd)
        for rnd in range(ROUNDS):
            scan(7, 1, rnd)
            attend(0, rnd)
            attention_rows(1, rnd)
            split_ahead(9, rnd)
        with act.Fori(2, HEADS) as h:
            for rnd in range(ROUNDS):
                attend(h - 1, rnd)
                attention_rows(h, rnd)
                split_ahead(h + 8, rnd)

        def mix(m, rnd):
            if rnd in (4, 8):
                j = rnd // 4 - 1
                arrived(m + 16, j)
                if not before_first(m - 1):
                    act.wait_ge(*mix_dve.at("ya", m - 1))
                act.activation(th[:, j, :], bank(proj_bank(j)), ACT.Tanh, scale=0.5).then_inc(*mix_act.inc(("ta", "tb")[j]))
                act.wait_ge(*mix_act.at(("ta", "tb")[j], m))
                act.sem_inc(bank_free[proj_bank(j)], 1)
            elif rnd == 15:
                act.wait_ge(*mix_dve.at("ys", m))
                act.activation(y_hi[:, bass.ds(m, 1), :] if not isinstance(m, int) else y_hi[:, m:m + 1, :],
                               ysum[:, 0:1, :], ACT.Copy, scale=0.5).then_inc(*mix_act.inc("yhi"))

        for rnd in range(ROUNDS):
            if rnd < 8:
                attend(7, rnd)
            if rnd == 8:
                act.wait_ge(*scan_dve.at("og", 7))
                act.wait_ge(*attend_act.at("pc3", 7))
                act.wait_ge(*attend_dve.at("oa", 7))
                for name, hi, full in (("ob", ob_hi, ob), ("oa", oa_hi, oa)):
                    for n in range(2):
                        act.activation(hi[:, n * half:(n + 1) * half, :], full[:, n * half:(n + 1) * half, :],
                                       ACT.Copy).then_inc(*parts_act.inc(f"{name}_hi{n}"))
            mix(0, rnd)
            split_ahead(16, rnd)
        with act.Fori(1, KT) as m:
            for rnd in range(ROUNDS):
                mix(m, rnd)
                split_ahead(m + 16, rnd)
        for n in range(2, 8):
            slot = (1 + n) % RING
            split(Q_OUT + n, slot, raw_value(slot, (U_OUT + n) // RING))
        for t in range(NT):
            act.wait_ge(*norm_pe.at(f"t{t}"))
            act.activation(oscr[:, t, :], ps[:, 2 * t:2 * t + 2, :], ACT.Square,
                           accum_out=small_cols[:, t:t + 1]).then_inc(*norm_act.inc(f"sq{t}"))

    @block.gpsimd
    def _(pool):
        scan_pool.count_ahead(pool)

        def split(q, slot, raw_at, n=P):
            pool.wait_ge(hi_made, q + 1)
            pool.tensor_tensor(w_lo[:, slot, :, 0:n], raw[:, slot, :, 0:n], w_hi[:, slot, :, 0:n].bitcast(F32),
                               ALU.subtract).then_inc(lo_made, 1)

        def split_ahead(it, rnd):
            if rnd % 4 == 1:
                j = rnd // 4 + 2
                split(q_of(it, j), (1 + j) % RING, None)

        pool.memset(nhalf[:], -0.5).then_inc(*pro_pool.inc("half"))
        pool.memset(eps_k[:], 4.0 * EPS).then_inc(*pro_pool.inc("eps_k"))
        pool.memset(eps_o[:], EPS * HD * HD).then_inc(*pro_pool.inc("eps_o"))
        pool.wait_ge(*pro_pool.at("eps_o"))
        pool.wait_ge(s_x, 16)
        for i in range(NT):
            pool.wait_ge(*pro_act.at(f"ssq{i}"))
        pool.tensor_scalar(small_cols[:, 4:8], small_cols[:, 0:4], 1.0 / D, EPS, ALU.mult, ALU.add).then_inc(
            *pro_pool.inc("ms"))
        pool.wait_ge(*pro_pool.at("ms"))
        pool.tensor_tensor(small_cols[:, 4:8], small_cols[:, 4:8], nhalf[:, 0:4], ALU.pow).then_inc(*pro_pool.inc("rstd"))
        pool.wait_ge(*pro_act.at("cos"))
        pool.wait_ge(*pro_act.at("sinI"))
        split(0, 0, None, N_SMALL)
        split(1, 1, None)
        pool.wait_ge(*pro_pe.at("mod"))
        pool.wait_ge(*pro_dve.at("m15"))
        pool.wait_ge(*pro_dve.at("lo7"))
        pool.wait_ge(*pro_act.at("hi7"))
        pool.wait_ge(lo_made, 2)
        pool.memset(kpad[64:P, 0, :], 0.0).then_inc(*pro_pool.inc("kpadE"))
        pool.wait_ge(*pro_pool.at("kpadE"))
        pool.memset(kpad[0:64, 1, :], 0.0).then_inc(*pro_pool.inc("kpadO"))
        pool.memset(rows[:, :, 0:3], 0.0).then_inc(*pro_pool.inc("pad"))
        split(2, 2, None)
        pool.wait_ge(*idx_dve.at("var"))
        pool.tensor_scalar(small_cols[:, 40:44], small_cols[:, 36:40], 1.0 / IDX_DIM, EPS, ALU.mult, ALU.add).then_inc(
            *idx_pool.inc("ms"))
        pool.wait_ge(*idx_pool.at("ms"))
        pool.tensor_tensor(small_cols[:, 40:44], small_cols[:, 40:44], nhalf[:, 0:4], ALU.pow).then_inc(
            *idx_pool.inc("rstd"))
        split(3, 3, None)
        split(4, 0, None)
        for n in range(4):
            pool.wait_ge(*idx_dve.at(f"sh{n}"))
            pool.wait_ge(*idx_act.at(f"q{n}"))
            pool.tensor_tensor(iq[:, n, :], iq[:, n, :], tab_cos[:, 1, :], ALU.mult).then_inc(*idx_pool.inc(f"cc{n}"))
        split(5, 1, None)
        split(6, 2, None)

        def prepare(h, par, rnd):
            s1, s2 = sst[:, par, 0:4].unsqueeze(2), sst[:, par, 4:8].unsqueeze(2)
            rk = st8[:, par, 0:4]
            if rnd == 15:
                if before_first(h - 1):
                    pool.wait_ge(*idx_dve.at("gp"))
                else:
                    pool.wait_ge(*solve_pe.at("Z64", h - 1))
                pool.tensor_copy(L[:], gh(G, h)).then_inc(*solve_pool.inc("gbt"))
                pool.wait_ge(*solve_act.at("k3", h))
                pool.tensor_tensor(rk, rk, eps_k[:, 0:4], ALU.add).then_inc(*solve_pool.inc("msk"))
                pool.wait_ge(*solve_pool.at("msk", h))
                pool.tensor_tensor(rk, rk, nhalf[:, 0:4], ALU.pow).then_inc(*solve_pool.inc("rnk"))
                pool.wait_ge(*solve_pool.at("rnk", h))
                if not before_first(h - 1):
                    pool.wait_ge(*solve_dve.at("kd", h - 1))
                pool.tensor_tensor(s1, rk.unsqueeze(2), gflat(BEGC, h), ALU.mult).then_inc(*solve_pool.inc("sbe"))
                pool.tensor_tensor(s2, rk.unsqueeze(2), gflat(EKD, h), ALU.mult).then_inc(*solve_pool.inc("skd"))

        def solve(h, par, rnd):
            if rnd == 0:
                pool.wait_ge(*solve_act.at("dec", h))
                pool.tensor_tensor(yy[:, 0, :, :], yy[:, 0, :, :], over_tiles(C_LOW), ALU.mult).then_inc(
                    *solve_pool.inc("mlow"))
                pool.wait_ge(*solve_pool.at("mlow", h))
                pool.tensor_tensor(yy[:, 0, :, :], yy[:, 0, :, :], gh(BETA, h), ALU.mult).then_inc(
                    *solve_pool.inc("beta"))
                pool.tensor_tensor(yy[:, 1, :, :], yy[:, 1, :, :], over_tiles(C_TRIU), ALU.mult).then_inc(
                    *solve_pool.inc("mup"))
            elif rnd == 2:
                rq = st8[:, par, 4:8]
                pool.wait_ge(*solve_act.at("q3", h))
                pool.tensor_tensor(rq, rq, eps_k[:, 4:8], ALU.add).then_inc(*solve_pool.inc("msq"))
                pool.wait_ge(*solve_pool.at("msq", h))
                pool.tensor_tensor(rq, rq, nhalf[:, 4:8], ALU.pow).then_inc(*solve_pool.inc("rnq"))
                if not before_first(h - 2):
                    pool.wait_ge(*scan_pe.at("O3", h - 2))
                pool.tensor_tensor(qe[:, par, :], y3[:, 0, :], E[:], ALU.mult).then_inc(*solve_pool.inc("qe"))

        def scan(h, par, rnd):
            if rnd == 10:
                pool.wait_ge(*scan_act.at("so3", h))
                if not before_first(h - 1):
                    pool.wait_ge(*scan_dve.at("on", h - 1))
                pool.wait_ge(*solve_pool.at("rnq", h))
                rq = st8[:, par, 4:8]
                pool.tensor_tensor(fo[:, 1, :], rq, rq, ALU.mult).then_inc(*scan_pool.inc("r2"))
                pool.wait_ge(*scan_pool.at("r2", h))
                pool.tensor_tensor(fo[:, 1, :], fo[:, 1, :], fo[:, 0, :], ALU.mult).then_inc(*scan_pool.inc("ms"))
                pool.wait_ge(*scan_pool.at("ms", h))
                pool.tensor_tensor(fo[:, 1, :], fo[:, 1, :], eps_o[:], ALU.add).then_inc(
                    *scan_pool.inc("ms2"))
                pool.wait_ge(*scan_pool.at("ms2", h))
                pool.tensor_tensor(fo[:, 1, :], fo[:, 1, :], nhalf[:, 0:4], ALU.pow).then_inc(*scan_pool.inc("rs"))
                pool.wait_ge(*scan_pool.at("rs", h))
                pool.tensor_tensor(fo[:, 2, :], fo[:, 1, :], rq, ALU.mult).then_inc(*scan_pool.inc("f"))

        def rope(h, rnd):
            if rnd == 12:
                pool.wait_ge(*rope_dve.at("sh", h))
                pool.tensor_tensor(qk[0:32, :, :], qk[0:32, :, :], tab_cos[0:32, 0:1, :].to_broadcast([32, 2, S]),
                                   ALU.mult).then_inc(*rope_pool.inc("cc"))

        for rnd in range(ROUNDS):
            split_ahead(0, rnd)
            prepare(0, 0, rnd)
        for rnd in range(ROUNDS):
            solve(0, 0, rnd)
            split_ahead(1, rnd)
            prepare(1, 1, rnd)
        with pool.Fori(0, 3) as pair:
            for par in range(2):
                h = pair * 2 + (2 + par)
                for rnd in range(ROUNDS):
                    solve(h - 1, 1 - par, rnd)
                    scan(h - 2, par, rnd)
                    split_ahead(h, rnd)
                    prepare(h, par, rnd)
        for rnd in range(ROUNDS):
            solve(7, 1, rnd)
            scan(6, 0, rnd)
            rope(0, rnd)
            split_ahead(8, rnd)
        for rnd in range(ROUNDS):
            scan(7, 1, rnd)
            rope(1, rnd)
            split_ahead(9, rnd)
        with pool.Fori(2, HEADS) as h:
            for rnd in range(ROUNDS):
                rope(h, rnd)
                split_ahead(h + 8, rnd)
        with pool.Fori(0, KT) as m:
            for rnd in range(ROUNDS):
                split_ahead(m + 16, rnd)
        for n in range(2, 8):
            split(Q_OUT + n, (1 + n) % RING, None)
        for t in range(NT):
            pool.wait_ge(*norm_act.at(f"sq{t}"))
            pool.tensor_scalar(small_cols[:, 8 + t:9 + t], small_cols[:, t:t + 1], 1.0 / D, EPS, ALU.mult,
                               ALU.add).then_inc(*norm_pool.inc(f"ms{t}"))
            pool.wait_ge(*norm_pool.at(f"ms{t}"))
            pool.tensor_tensor(small_cols[:, 8 + t:9 + t], small_cols[:, 8 + t:9 + t], nhalf[:, 0:1], ALU.pow).then_inc(
                *norm_pool.inc(f"rs{t}"))

    @block.vector
    def _(dve):
        scan_dve.count_ahead(dve)

        dve.wait_ge(*pro_pe.at("rows2T"))
        dve.tensor_copy(pcol[:, 0, :], ps[:, 2, 0:P]).then_inc(*pro_dve.inc("pcol"))
        dve.tensor_copy(pcol[:, 1, 0:3], ps[:, 2, P:P + 3]).then_inc(*pro_dve.inc("pcol2"))
        dve.wait_ge(*pro_dve.at("pcol"))
        dve.tensor_copy(cb[:], pcol[:, 0, R_C:R_C + KT].unsqueeze(2).to_broadcast([P, KT, P])).then_inc(*pro_dve.inc("cb"))
        dve.wait_ge(*pro_dve.at("pcol2"))
        dve.tensor_scalar(small_cols[:, 44:45], pcol[:, 1, R2_NG:R2_NG + 1], 0.5, None, ALU.mult).then_inc(
            *pro_dve.inc("hgain"))
        dve.wait_ge(s_pos, 16)
        dve.tensor_copy(pos_f[:], pos_i[:]).then_inc(*pro_dve.inc("posf"))
        dve.wait_ge(*pro_dve.at("posf"))
        ang, turns, r, rc = (rp[:, n, :] for n in range(4))
        for t, name in ((0, "angA"), (1, "angI")):
            dve.tensor_scalar(rp[:, 0, t * S:(t + 1) * S], pos_f[:], cols[:, t:t + 1], None, ALU.mult).then_inc(
                *pro_dve.inc(name))
        dve.wait_ge(*pro_dve.at("angI"))
        magic = 1.5 * 2.0 ** 23
        dve.tensor_scalar(turns, ang, 1.0 / (2 * np.pi), magic, ALU.mult, ALU.add).then_inc(*pro_dve.inc("turns"))
        dve.wait_ge(*pro_dve.at("turns"))
        dve.tensor_scalar(turns, turns, magic, None, ALU.subtract).then_inc(*pro_dve.inc("whole"))
        c1 = 6.28125
        c2 = float(np.float32(np.round((2 * np.pi - c1) * 2.0 ** 22) / 2.0 ** 22))
        c3 = float(np.float32(2 * np.pi - c1 - c2))
        dve.wait_ge(*pro_dve.at("whole"))
        dve.scalar_tensor_tensor(out=r, in0=turns, scalar=-c1, in1=ang, op0=ALU.mult, op1=ALU.add).then_inc(
            *pro_dve.inc("r1"))
        for n, cc in ((2, c2), (3, c3)):
            dve.wait_ge(*pro_dve.at(f"r{n - 1}"))
            dve.scalar_tensor_tensor(out=r, in0=turns, scalar=-cc, in1=r, op0=ALU.mult, op1=ALU.add).then_inc(
                *pro_dve.inc(f"r{n}"))
        dve.wait_ge(*pro_dve.at("r3"))
        dve.tensor_scalar(rc, r, np.pi / 2, None, ALU.add).then_inc(*pro_dve.inc("rc"))
        dve.wait_ge(*pro_dve.at("rc"))
        dve.tensor_scalar(turns, rc, np.pi, -2 * np.pi, ALU.is_gt, ALU.mult).then_inc(*pro_dve.inc("wrap"))
        dve.wait_ge(*pro_dve.at("wrap"))
        dve.tensor_tensor(rc, rc, turns, ALU.add).then_inc(*pro_dve.inc("rc2"))
        pi = float(np.nextafter(np.float32(np.pi), np.float32(0)))
        dve.tensor_scalar(r, r, -pi, pi, ALU.max, ALU.min).then_inc(*pro_dve.inc("clamp"))
        dve.wait_ge(*pro_dve.at("rc2"))
        dve.tensor_scalar(rc, rc, -pi, pi, ALU.max, ALU.min).then_inc(*pro_dve.inc("clampc"))
        dve.wait_ge(*pro_pool.at("rstd"))
        for i in range(NT):
            dve.tensor_scalar(x_sb[:, i, :], x_sb[:, i, :], small_cols[:, 4 + i:5 + i], None, ALU.mult).then_inc(
                *pro_dve.inc(f"xn{i}"))
        for k in range(0, KT, 2):
            dve.wait_ge(*pro_pe.at(f"x{k}"))
            if k == 0:
                dve.wait_ge(*pro_act.at("ssq3"))
            dve.tensor_copy(xT[:, k, :], ps[:, [0, 1, 6, 7][k % 4], :]).then_inc(*pro_dve.inc(f"x{k}"))
        dve.wait_ge(*pro_pe.at("mod"))
        for b in range(16):
            dve.tensor_tensor_reduce(scratch16[:, b, :], ps[:, 2 + b // 4, blk(b % 4)], ident, 1.0, 0.0, ALU.mult, ALU.add,
                                     small_cols[:, 8 + b:9 + b]).then_inc(*pro_dve.inc(f"m{b}"))
        dve.wait_ge(*pro_dve.at("m15"))
        dve.tensor_tensor(small_cols[:, 8:24], small_cols[:, 8:24], pcol[:, 0, R_BADA:R_BADA + 16], ALU.add).then_inc(
            *pro_dve.inc("mb"))
        dve.wait_ge(*pro_dve.at("mb"))
        dve.scalar_tensor_tensor(out=small_cols[:, 24:32], in0=small_cols[:, 16:24], scalar=1.0,
                                 in1=pcol[:, 0, R_GAIN:R_GAIN + 8], op0=ALU.add, op1=ALU.mult).then_inc(*pro_dve.inc("scg"))
        dve.wait_ge(*pro_dve.at("scg"))
        for k in range(KT + 1):
            if k < KT:
                dve.wait_ge(*(pro_dve if k % 2 == 0 else pro_act).at(f"x{k}"))
                dve.tensor_scalar(xT[:, k, :], xT[:, k, :], small_cols[:, 24 + k:25 + k], small_cols[:, 8 + k:9 + k],
                                  ALU.mult, ALU.add).then_inc(*pro_dve.inc(f"h{k}"))
            if k > 0:
                dve.wait_ge(*pro_act.at(f"hi{k - 1}"))
                dve.tensor_tensor(h_lo[:, k - 1, :], xT[:, k - 1, :], h_hi[:, k - 1, :].bitcast(F32),
                                  ALU.subtract).then_inc(*pro_dve.inc(f"lo{k - 1}"))

        dve.wait_ge(*idx_pe.at("smT"))
        dve.tensor_copy(sm[:], tiles(bank(2))[:, :, 0:N_SMALL]).then_inc(*idx_dve.inc("sm"))
        dve.wait_ge(*idx_dve.at("sm"))
        dve.tensor_reduce(small_cols[:, 32:36], sm[:, :, 0:IDX_DIM], AX_X, ALU.add).then_inc(*idx_dve.inc("mu"))
        dve.wait_ge(*idx_dve.at("mu"))
        dve.tensor_scalar(small_cols[:, 32:36], small_cols[:, 32:36], 1.0 / IDX_DIM, None, ALU.mult).then_inc(
            *idx_dve.inc("mus"))
        dve.wait_ge(*idx_dve.at("mus"))
        dve.tensor_tensor(cent[:], sm[:, :, 0:IDX_DIM], per_tile(small_cols[:, 32:36], IDX_DIM), ALU.subtract).then_inc(
            *idx_dve.inc("cent"))
        dve.wait_ge(*idx_dve.at("cent"))
        dve.tensor_tensor(csq[:], cent[:], cent[:], ALU.mult).then_inc(*idx_dve.inc("csq"))
        dve.wait_ge(*idx_dve.at("csq"))
        dve.tensor_reduce(small_cols[:, 36:40], csq[:], AX_X, ALU.add).then_inc(*idx_dve.inc("var"))
        dve.tensor_scalar(sm[:, :, SM_IW:SM_IW + IDX_HEADS], sm[:, :, SM_IW:SM_IW + IDX_HEADS], IDX_HEADS ** -0.5, None,
                          ALU.mult).then_inc(*idx_dve.inc("iw"))
        dve.wait_ge(s_sc, 32)
        dve.tensor_tensor(gsc[:, G, :, :], sm[:, :, SM_DECAY:SM_DECAY + HEADS],
                          small_cols[:, 56:64].unsqueeze(1).to_broadcast([P, NT, HEADS]), ALU.add).then_inc(*idx_dve.inc("z"))
        dve.wait_ge(*idx_dve.at("z"))
        dve.scalar_tensor_tensor(out=gsc[:, EKD, :, :], in0=gsc[:, G, :, :], scalar=-1.0, in1=gsc[:, G, :, :], op0=ALU.mult,
                                 op1=ALU.max).then_inc(*idx_dve.inc("az"))
        dve.wait_ge(*idx_pool.at("rstd"))
        for n in range(2):
            dve.tensor_tensor(kdup[:, :, n * IDX_DIM:(n + 1) * IDX_DIM], cent[:], per_tile(small_cols[:, 40:44], IDX_DIM),
                              ALU.mult).then_inc(*idx_dve.inc(f"kd{n}"))
        dve.wait_ge(*idx_act.at("tanh"))
        dve.tensor_scalar(gsc[:, BETA, :, :], gsc[:, TMP, :, :], 0.5, 0.5, ALU.mult, ALU.add).then_inc(*idx_dve.inc("beta"))
        dve.wait_ge(*idx_act.at("ab"))
        dve.tensor_scalar(gsc[:, EGC, :, :], gsc[:, EGC, :, :], 1.0, None, ALU.add).then_inc(*idx_dve.inc("sp1"))
        dve.wait_ge(*idx_act.at("ln"))
        dve.scalar_tensor_tensor(out=gsc[:, G, :, :], in0=gsc[:, G, :, :], scalar=0.0, in1=gsc[:, EGC, :, :], op0=ALU.max,
                                 op1=ALU.add).then_inc(*idx_dve.inc("sp"))
        dve.wait_ge(*idx_dve.at("sp"))
        dve.wait_ge(*idx_act.at("na"))
        dve.scalar_tensor_tensor(out=gsc[:, G, :, :], in0=gsc[:, G, :, :], scalar=-1.0,
                                 in1=small_cols[:, 48:56].unsqueeze(1).to_broadcast([P, NT, HEADS]), op0=ALU.mult,
                                 op1=ALU.mult).then_inc(*idx_dve.inc("g"))
        swap_idx = [(i + 8) % 16 if i < 16 else i for i in range(32)]
        for n in range(4):
            dve.wait_ge(*idx_act.at(f"q{n}"))
            dve.stream_shuffle(isw[:, n, :], iq[:, n, :], mask=swap_idx).then_inc(*idx_dve.inc(f"sh{n}"))
            dve.wait_ge(*idx_dve.at(f"sh{n}"))
            dve.tensor_tensor(isw[:, n, :], isw[:, n, :], tab_sin[:, 1, :], ALU.mult).then_inc(*idx_dve.inc(f"ss{n}"))
        dve.wait_ge(*idx_pe.at("kT"))
        dve.tensor_scalar(kx[:], bank(3), pcol[:, 1, R2_LNG:R2_LNG + 1], pcol[:, 1, R2_LNB:R2_LNB + 1], ALU.mult,
                          ALU.add).then_inc(*idx_dve.inc("kx"))
        dve.wait_ge(*idx_dve.at("kx"))
        dve.stream_shuffle(ksw[:], kx[:], mask=swap_idx).then_inc(*idx_dve.inc("ksh"))
        dve.wait_ge(*idx_dve.at("ksh"))
        dve.tensor_tensor(ksw[:], ksw[:], tab_sin[:, 1, :], ALU.mult).then_inc(*idx_dve.inc("kss"))
        dve.tensor_tensor(kx[:], kx[:], tab_cos[:, 1, :], ALU.mult).then_inc(*idx_dve.inc("kcc"))
        dve.wait_ge(*idx_dve.at("kcc"))
        dve.wait_ge(*pro_pool.at("kpadO"))
        dve.tensor_tensor(kpad[0:64, 0, :], kx[0:64, :], ksw[0:64, :], ALU.add).then_inc(*idx_dve.inc("kE"))
        dve.tensor_tensor(kpad[64:P, 1, :], kx[64:P, :], ksw[64:P, :], ALU.add).then_inc(*idx_dve.inc("kO"))
        dve.wait_ge(*idx_pe.at("gl"))
        dve.tensor_copy(gsc[:, GC:GL + 1, :, :].rearrange("p a i h -> p (a i h)"), ps[:, 4, 0:2 * NT * HEADS]).then_inc(
            *idx_dve.inc("gc"))
        dve.wait_ge(*idx_dve.at("gc"))
        dve.tensor_tensor(gsc[:, TMP, :, :], gsc[:, GL, :, :], gsc[:, GC, :, :], ALU.subtract).then_inc(*idx_dve.inc("dkd"))
        dve.wait_ge(*idx_act.at("egc"))
        dve.tensor_tensor(gsc[:, BEGC, :, :], gsc[:, BETA, :, :], gsc[:, EGC, :, :], ALU.mult).then_inc(
            *idx_dve.inc("begc"))
        dve.tensor_scalar(gsc[:, HBETA, :, :], gsc[:, BETA, :, :], 0.5, None, ALU.mult).then_inc(*idx_dve.inc("hbeta"))
        for n in range(4):
            dve.wait_ge(*idx_pool.at(f"cc{n}"))
            dve.wait_ge(*idx_dve.at(f"ss{n}"))
            dve.tensor_tensor(iq[:, n, :], iq[:, n, :], isw[:, n, :], ALU.add).then_inc(*idx_dve.inc(f"ad{n}"))
        for hd in range(8):
            for qt in (1, 2, 3):
                m = 3 * hd + qt - 1
                n = (qt + 1) * P
                w = sm[:, qt, SM_IW + hd:SM_IW + hd + 1]
                dve.wait_ge(*idx_act.at(f"r{hd}_{qt}"))
                if hd == 0:
                    ins = dve.tensor_scalar(score[:, qt, 0:n], relu[:, m % 4, 0:n], w, None, ALU.mult)
                else:
                    dve.wait_ge(*idx_dve.at(f"s{hd - 1}_{qt}"))
                    ins = dve.scalar_tensor_tensor(out=score[:, qt, 0:n], in0=relu[:, m % 4, 0:n], scalar=w,
                                                   in1=score[:, qt, 0:n], op0=ALU.mult, op1=ALU.add)
                ins.then_inc(*idx_dve.inc(f"s{hd}_{qt}"))
        for qt in (1, 2, 3):
            dve.wait_ge(*idx_dve.at(f"s7_{qt}"))
            dve.tensor_tensor(score[:, qt, blk(qt)], score[:, qt, blk(qt)], cst[:, C_TRIL, :], ALU.mult).then_inc(
                *idx_dve.inc(f"tril{qt}"))
            dve.wait_ge(*idx_dve.at(f"tril{qt}"))
            dve.tensor_tensor(score[:, qt, blk(qt)], score[:, qt, blk(qt)], cst[:, C_FILL, :], ALU.add).then_inc(
                *idx_dve.inc(f"fill{qt}"))
        dve.tensor_copy(score[:, 0, 0:P], cst[:, C_MASKED, :]).then_inc(*idx_dve.inc("m0"))
        dve.wait_ge(s_bc, 32)
        dve.wait_ge(*idx_act.at("gate7"))
        dve.tensor_tensor(gate[:], gate[:], bgate[:], ALU.add).then_inc(*idx_dve.inc("gb"))
        dve.wait_ge(*idx_dve.at("gb"))
        dve.tensor_tensor(gate[:], gate[:], pgain[:], ALU.mult).then_inc(*idx_dve.inc("gp"))

        def solve(h, par, rnd):
            if rnd == 0:
                dve.wait_ge(*solve_pe.at("k", h))
                dve.wait_ge(*solve_pool.at("rnk", h))
                if not before_first(h - 1):
                    dve.wait_ge(*solve_pe.at("dU64", h - 1))
                dve.tensor_tensor(kn[:], tiles(bank(5)), per_tile(st8[:, par, 0:4]), ALU.mult).then_inc(
                    *solve_dve.inc("kn"))
                dve.wait_ge(*solve_pe.at("P", h))
                dve.wait_ge(*solve_act.at("E", h))
                dve.tensor_tensor(yy[:, 0, :, :], tiles(bank(2)), gh(GC, h), ALU.subtract).then_inc(
                    *solve_dve.inc("y1"))
                dve.wait_ge(*solve_dve.at("y1", h))
                dve.tensor_scalar(yy[:, 1, :, :], yy[:, 0, :, :], 0.0, None, ALU.min).then_inc(*solve_dve.inc("yup"))
                dve.wait_ge(*solve_dve.at("yup", h))
                dve.tensor_scalar(yy[:, 0, :, :], yy[:, 0, :, :], 0.0, -1.0, ALU.max, ALU.mult).then_inc(
                    *solve_dve.inc("ylo"))
                if not before_first(h - 2):
                    dve.wait_ge(*scan_pe.at("O3", h - 2))
                dve.wait_ge(*solve_pool.at("skd", h))
                dve.tensor_tensor(kbe[:, par], tiles(bank(5)), per_tile(sst[:, par, 0:4]), ALU.mult).then_inc(
                    *solve_dve.inc("kbe"))
                dve.tensor_tensor(kd[:, par], tiles(bank(5)), per_tile(sst[:, par, 4:8]), ALU.mult).then_inc(
                    *solve_dve.inc("kd"))
            elif rnd == 1:
                dve.wait_ge(*solve_pe.at("v", h))
                dve.tensor_tensor(vb[:, par], tiles(bank(3)), gh(HBETA, h), ALU.mult).then_inc(*solve_dve.inc("vb"))
            elif rnd == 2:
                dve.wait_ge(*solve_pe.at("gram", h))
                dve.wait_ge(*solve_pool.at("beta", h))
                dve.tensor_tensor(L[:], tiles(bank(5)), yy[:, 0], ALU.mult).then_inc(*solve_dve.inc("L"))
                dve.wait_ge(*solve_pe.at("qk", h))
                dve.wait_ge(*solve_pool.at("mup", h))
                dve.tensor_tensor(intra[:, par], tiles(bank(4)), yy[:, 1], ALU.mult).then_inc(*solve_dve.inc("A"))
            elif rnd == 3:
                dve.wait_ge(*solve_dve.at("L", h))
                dve.tensor_tensor(T[:], L[:], over_tiles(C_NEG1LOW), ALU.mult).then_inc(*solve_dve.inc("T0"))
                dve.wait_ge(*solve_dve.at("T0", h))
                dve.tensor_tensor(T[:], T[:], over_tiles(C_ID), ALU.add).then_inc(*solve_dve.inc("T1"))
                dve.wait_ge(*solve_pe.at("LT", h))
                dve.tensor_tensor(U[:, par], tiles(bank(3)), over_tiles(C_NEG), ALU.mult).then_inc(*solve_dve.inc("U0"))
                dve.wait_ge(*solve_dve.at("U0", h))
                dve.tensor_tensor(U[:, par], U[:, par], over_tiles(C_ID), ALU.add).then_inc(*solve_dve.inc("U1"))
            elif rnd % 2 == 0 and rnd >= 4:
                s = LEVELS[rnd // 2 - 1]
                dve.wait_ge(*solve_pe.at(f"Z{s}", h))
                dve.tensor_tensor(kn[:], tiles(bank(2)), over_tiles(C_NEG + rnd // 2 - 1), ALU.mult).then_inc(
                    *solve_dve.inc(f"Z{s}"))
            elif rnd >= 5:
                s = LEVELS[rnd // 2 - 1]
                dve.wait_ge(*solve_pe.at(f"dU{s}", h))
                dve.tensor_tensor(U[:, par], U[:, par], tiles(bank(3)), ALU.add).then_inc(*solve_dve.inc(f"U{s}"))
                if s < 64:
                    dve.wait_ge(*solve_pe.at(f"dT{s}", h))
                    dve.tensor_tensor(T[:], T[:], tiles(bank(4)), ALU.add).then_inc(*solve_dve.inc(f"T{s}"))

        def scan(h, par, rnd):
            if 1 <= rnd <= 8 and rnd % 2 == 1:
                i = rnd // 2
                dve.wait_ge(*scan_pe.at(f"V{i}", h))
                dve.tensor_copy(vnew[:], ps[:, 6, 0:P]).then_inc(*scan_dve.inc(f"vn{i}"))
            elif 1 <= rnd <= 8 and rnd % 2 == 0 and rnd < 8:
                i = rnd // 2 - 1
                dve.wait_ge(*scan_pe.at(f"S{i}", h))
                if i == 0:
                    ins = dve.tensor_copy(state[:], ps[:, 7, 0:P])
                else:
                    dve.wait_ge(*scan_dve.at(f"st{i - 1}", h))
                    ins = dve.scalar_tensor_tensor(out=state[:], in0=state[:], scalar=gcol(EGL, h, i), in1=ps[:, 7, 0:P],
                                                   op0=ALU.mult, op1=ALU.add)
                ins.then_inc(*scan_dve.inc(f"st{i}"))
            elif rnd == 11:
                dve.wait_ge(*scan_pool.at("f", h))
                dve.scalar_tensor_tensor(out=o_tok[:], in0=o_tok[:], scalar=HD ** 0.5, in1=per_tile(fo[:, 2, :]),
                                         op0=ALU.mult, op1=ALU.mult).then_inc(*scan_dve.inc("on"))
            elif rnd == 13:
                dve.wait_ge(*scan_pe.at("oT", h))
                dve.scalar_tensor_tensor(out=head_slot(ob, h), in0=bank(7), scalar=small_cols[:, 44:45], in1=zb[:, par, :],
                                         op0=ALU.mult, op1=ALU.mult).then_inc(*scan_dve.inc("og"))

        def select(h, rnd):
            where = {2: (0, 0), 3: (0, 1), 4: (0, 2), 7: (1, 0), 11: (1, 1), 12: (1, 2)}
            if rnd in where:
                n, t = where[rnd]
                w = score[:, t + 1, 0:(t + 2) * P]
                if n == 0:
                    if not before_first(h - 1):
                        dve.wait_ge(*top_dve.at(f"take{t}1", h - 1))
                    if before_first(h - 1):
                        dve.wait_ge(*idx_dve.at(f"fill{t + 1}"))
                else:
                    dve.wait_ge(*top_dve.at(f"take{t}0", h))
                passed(dve)
                dve.max(m8[:, t, :], w).then_inc(*top_dve.inc(f"max{t}{n}"))
                dve.wait_ge(*top_dve.at(f"max{t}{n}", h))
                passed(dve)
                dve.match_replace(w, m8[:, t, :], w, TAKEN).then_inc(*top_dve.inc(f"take{t}{n}"))

        def convolve(h, par, rnd):
            for j, (name, at) in enumerate((("q", 6), ("k", 10), ("v", 14))):
                if rnd == at:
                    dve.wait_ge(*conv_act.at(f"tap_{name}", h))
                    if isinstance(h, int) and h == 0:
                        dve.wait_ge(*pro_pool.at("pad"))
                    for n in (1, 2, 3):
                        if n > 1:
                            dve.wait_ge(*conv_dve.at(f"{name}{n - 1}", h))
                        dve.scalar_tensor_tensor(out=y3[:, j, :], in0=rows[:, j, 3 - n:3 - n + S],
                                                 scalar=pcol_at(R_CONV + (3 - n) * 24 + j * 8, h), in1=y3[:, j, :],
                                                 op0=ALU.mult, op1=ALU.add).then_inc(*conv_dve.inc(f"{name}{n}"))
            for j, (name, at) in enumerate((("q", 9), ("k", 13), ("v", 15))):
                if rnd == at:
                    dve.wait_ge(*conv_act.at(f"tanh_{name}", h))
                    dve.scalar_tensor_tensor(out=y3[:, j, :], in0=tz[:], scalar=1.0, in1=y3[:, j, :], op0=ALU.add,
                                             op1=ALU.mult).then_inc(*conv_dve.inc(f"{name}s"))

        def gate_z(h, par, rnd):
            if rnd == 1:
                dve.wait_ge(*conv_act.at("tanh_z", h))
                if not before_first(h - 2):
                    dve.wait_ge(*scan_dve.at("og", h - 2))
                dve.scalar_tensor_tensor(out=zb[:, par, :], in0=tz[:], scalar=1.0, in1=zraw[:], op0=ALU.add,
                                         op1=ALU.mult).then_inc(*conv_dve.inc("zs"))

        def rope(h, rnd):
            if rnd == 11:
                dve.wait_ge(*a_act.at("k", h))
                if isinstance(h, int) and h == 0:
                    dve.wait_ge(*conv_dve.at("vs", HEADS - 1))
                else:
                    if not before_first(h - 1):
                        dve.wait_ge(*rope_dve.at("ad", h - 1))
                passed(dve)
                dve.stream_shuffle(sw[:], qk[0:32, :, :], mask=[i ^ 16 for i in range(32)]).then_inc(*rope_dve.inc("sh"))
                dve.wait_ge(*rope_dve.at("sh", h))
                dve.tensor_tensor(sw[:], sw[:], tab_sin[0:32, 0:1, :].to_broadcast([32, 2, S]), ALU.mult).then_inc(
                    *rope_dve.inc("ss"))
            elif rnd == 14:
                dve.wait_ge(*rope_pool.at("cc", h))
                dve.wait_ge(*rope_dve.at("ss", h))
                dve.tensor_tensor(qk[0:32, :, :], qk[0:32, :, :], sw[:], ALU.add).then_inc(*rope_dve.inc("ad"))
            elif rnd == 15:
                dve.wait_ge(*a_act.at("tanh", h))
                dve.scalar_tensor_tensor(out=tz[:], in0=tz[:], scalar=1.0, in1=zraw[:], op0=ALU.add,
                                         op1=ALU.mult).then_inc(*rope_dve.inc("zs"))

        def attend(h, rnd):
            if rnd in (1, 2):
                for qt in (0, 1) if rnd == 1 else (2, 3):
                    n = (qt + 1) * P
                    dve.wait_ge(*attend_pe.at(f"s{qt}", h))
                    if qt == 0:
                        if not before_first(h - 1):
                            dve.wait_ge(*attend_pe.at("pt3", h - 1))
                        dve.wait_ge(*a_mask.at("m3"))
                    passed(dve)
                    dve.tensor_tensor_reduce(prob[:, qt, 0:n], ps[:, (3, 4, 5, 2)[qt], 0:n], score[:, qt, 0:n], 1.0,
                                             TAKEN, ALU.add, ALU.max, amx[:, 0, qt:qt + 1]).then_inc(
                        *attend_dve.inc(f"m{qt}"))
                if rnd == 2:
                    dve.wait_ge(*attend_dve.at("m3", h))
                    dve.tensor_scalar(amx[:, 1, :], amx[:, 0, :], -(HD ** -0.5), None, ALU.mult).then_inc(
                        *attend_dve.inc("nb"))
            elif rnd == 4:
                dve.wait_ge(*attend_act.at("e3", h))
                dve.reciprocal(amx[:, 3, :], amx[:, 2, :]).then_inc(*attend_dve.inc("rc"))
                dve.wait_ge(*attend_dve.at("rc", h))
                for qt in range(NT):
                    n = (qt + 1) * P
                    dve.tensor_scalar(prob[:, qt, 0:n], prob[:, qt, 0:n], amx[:, 3, qt:qt + 1], None, ALU.mult).then_inc(
                        *attend_dve.inc(f"p{qt}"))
            elif rnd == (13 if isinstance(h, int) and h == 0 else 8):
                dve.wait_ge(*attend_pe.at("pv", h))
                dve.wait_ge(*rope_dve.at("zs", h))
                if isinstance(h, int) and h == 0:
                    dve.wait_ge(*scan_dve.at("og", HEADS - 1))
                dve.scalar_tensor_tensor(out=head_slot(oa, h), in0=bank(3), scalar=0.5, in1=tz[:], op0=ALU.mult,
                                         op1=ALU.mult).then_inc(*attend_dve.inc("oa"))

        for rnd in range(ROUNDS):
            select(0, rnd)
            convolve(0, 0, rnd)
        for rnd in range(ROUNDS):
            solve(0, 0, rnd)
            gate_z(0, 0, rnd)
            select(1, rnd)
            convolve(1, 1, rnd)
        with dve.Fori(0, 3) as pair:
            for par in range(2):
                h = pair * 2 + (2 + par)
                for rnd in range(ROUNDS):
                    solve(h - 1, 1 - par, rnd)
                    scan(h - 2, par, rnd)
                    gate_z(h - 1, 1 - par, rnd)
                    select(h, rnd)
                    convolve(h, par, rnd)
        for qt in (1, 2, 3):
            n = (qt + 1) * P
            dve.wait_ge(*top_dve.at(f"take{qt - 1}1", HEADS - 1))
            dve.tensor_scalar(score[:, qt, 0:n], score[:, qt, 0:n], 2.0 * FILL, MASKED, ALU.is_gt, ALU.mult).then_inc(
                *a_mask.inc(f"m{qt}"))
        for rnd in range(ROUNDS):
            solve(7, 1, rnd)
            scan(6, 0, rnd)
            gate_z(7, 1, rnd)
            rope(0, rnd)
        for rnd in range(ROUNDS):
            scan(7, 1, rnd)
            attend(0, rnd)
            rope(1, rnd)
        with dve.Fori(2, HEADS) as h:
            for rnd in range(ROUNDS):
                attend(h - 1, rnd)
                rope(h, rnd)
        for rnd in range(10):
            attend(7, rnd)
        for n in range(2):
            dve.wait_ge(*parts_act.at(f"ob_hi{n}"))
            dve.tensor_tensor(ob_lo[n][:], ob[:, n * half:(n + 1) * half, :],
                              ob_hi[:, n * half:(n + 1) * half, :].bitcast(F32), ALU.subtract).then_inc(
                *parts_dve.inc(f"ob_lo{n}"))
        for n in range(2):
            dve.wait_ge(*parts_act.at(f"oa_hi{n}"))
            dve.tensor_tensor(oa_lo[:, n * half:(n + 1) * half, :], oa[:, n * half:(n + 1) * half, :],
                              oa_hi[:, n * half:(n + 1) * half, :].bitcast(F32), ALU.subtract).then_inc(
                *parts_dve.inc(f"oa_lo{n}"))

        def mix(m):
            dve.wait_ge(unit_done, q_of(m + 16, 2) + 1)
            dve.wait_ge(*mix_act.at("tb", m))
            if not before_first(m - 1):
                dve.wait_ge(*mix_dve.at("ylo", m - 1))
            b2, b3 = (1 + 2) % 2, (1 + 3) % 2
            dve.scalar_tensor_tensor(out=ysum[:, 1, :], in0=th[:, 1, :], scalar=1.0, in1=bank(b2), op0=ALU.add,
                                     op1=ALU.mult).then_inc(*mix_dve.inc("yb"))
            dve.wait_ge(*mix_dve.at("yb", m))
            dve.sem_inc(bank_free[b2], 1)
            dve.wait_ge(unit_done, q_of(m + 16, 3) + 1)
            if not before_first(m - 1):
                dve.wait_ge(*mix_act.at("yhi", m - 1))
            dve.scalar_tensor_tensor(out=ysum[:, 0, :], in0=th[:, 0, :], scalar=1.0, in1=bank(b3), op0=ALU.add,
                                     op1=ALU.mult).then_inc(*mix_dve.inc("ya"))
            dve.wait_ge(*mix_dve.at("ya", m))
            dve.sem_inc(bank_free[b3], 1)
            dve.tensor_tensor(ysum[:, 0, :], ysum[:, 0, :], ysum[:, 1, :], ALU.add).then_inc(*mix_dve.inc("ys"))
            dve.wait_ge(*mix_act.at("yhi", m))
            dve.scalar_tensor_tensor(out=head_slot(y_lo, m), in0=ysum[:, 0, :], scalar=0.5,
                                     in1=head_slot(y_hi, m).bitcast(F32), op0=ALU.mult, op1=ALU.subtract).then_inc(
                *mix_dve.inc("ylo"))

        mix(0)
        with dve.Fori(1, KT) as m:
            mix(m)
        dve.wait_ge(s_xres, 16)
        for t in range(NT):
            dve.wait_ge(*norm_pool.at(f"rs{t}"))
            dve.scalar_tensor_tensor(out=out_sb[:, t, :], in0=ps[:, 2 * t:2 * t + 2, :].rearrange("p a b -> p (a b)"),
                                     scalar=small_cols[:, 8 + t:9 + t], in1=gate[:], op0=ALU.mult, op1=ALU.mult).then_inc(
                *norm_dve.inc(f"n{t}"))
            dve.wait_ge(*norm_dve.at(f"n{t}"))
            dve.tensor_tensor(out_sb[:, t, :], out_sb[:, t, :], x_res[:, t, :], ALU.add).then_inc(*norm_dve.inc(f"x{t}"))


NAMES = ["x", "c", "positions", "w_ada", "b_ada", "pre_norm_gain", "post_norm_gain", "w_in", "idx_k_ln_gain",
         "idx_k_ln_bias", "dn_conv_w", "dn_a_log", "dn_dt_bias", "dn_norm_gain", "w_a_out", "w_b_out", "w_o"]


def kernel(**inputs):
    import concourse.bacc as bacc
    from concourse.bass_utils import run_bass_kernel_spmd

    nc = bacc.Bacc("TRN2", target_bir_lowering=False, num_devices=1)
    arrays, args = {}, []

    def add(name, a):
        a = np.ascontiguousarray(a)
        arrays[f"in_{name}"] = a
        args.append(nc.dram_tensor(f"in_{name}", a.shape, mybir.dt.from_np(a.dtype), kind="ExternalInput").ap())

    for name in NAMES:
        a = np.asarray(inputs[name])
        add(name, a if name in ("c", "positions") else a[0])
    for name, a in zip(("masks", "rotary"), constants()):
        add(name, a)
    args.append(nc.dram_tensor("out", (S, D), F32, kind="ExternalOutput").ap())
    build(nc, *args)
    r = run_bass_kernel_spmd(nc, [arrays], core_ids=[0])
    return r.results[0]["out"].reshape(1, S, D)
```
